# Optimizing a Trainium2 kernel written in Bass

```python
import numpy as np
import jax, jax.numpy as jnp
from jax import lax

D_MODEL = 1024
BATCH = 1
SEQ = 256
DEPTH = 1
DEC_BATCH = 8
DEC_SEQ = 8
PAST_LEN = 2048
PAGE_SIZE = 128

MIX_WIDTH = D_MODEL
RET_WIDTH = MIX_WIDTH // 2
RET_HEADS = 4
RET_HEAD_DIM = RET_WIDTH // RET_HEADS
MLSTM_WIDTH = MIX_WIDTH - RET_WIDTH
MLSTM_HEADS = 4
MLSTM_HEAD_DIM = MLSTM_WIDTH // MLSTM_HEADS
CONV_WIDTH = 4
CHUNK = 128
ROPE_BASE = 10000.0
N_EXPERTS = 32
TOP_K = 4
D_FF = D_MODEL
SWIGLU_LIMIT = 7.0
SWIGLU_ALPHA = 1.702
EXPERT_BLOCK = 128
N_MOD = 6
EPS = 1e-6
PROJ_SIZES = (RET_WIDTH, RET_WIDTH, RET_WIDTH, RET_WIDTH, 2 * MLSTM_WIDTH, MLSTM_WIDTH, MLSTM_WIDTH, MLSTM_HEADS, MLSTM_HEADS)
PROJ_COLS = sum(PROJ_SIZES)

kernel_name = 'hybrid_retention_mlstm_moe_step'

def rms_norm(x, g):
    xf = x.astype(jnp.float32)
    y = xf * lax.rsqrt(jnp.mean(xf * xf, axis=-1, keepdims=True) + EPS)
    return (y * g.astype(jnp.float32)).astype(x.dtype)

def head_norm(x, g):
    mu = jnp.mean(x, axis=-1, keepdims=True)
    xc = x - mu
    var = jnp.mean(xc * xc, axis=-1, keepdims=True)
    return xc * lax.rsqrt(var + EPS) * g.astype(jnp.float32)

def rotary(x, pos):
    half = x.shape[-1] // 2
    inv_freq = jnp.power(ROPE_BASE, -jnp.arange(half, dtype=jnp.float32) / half)
    ang = pos.astype(jnp.float32)[:, None] * inv_freq[None, :]
    cos = jnp.cos(ang)[None, :, None, :]
    sin = jnp.sin(ang)[None, :, None, :]
    x1, x2 = x[..., :half], x[..., half:]
    return jnp.concatenate([x1 * cos - x2 * sin, x2 * cos + x1 * sin], axis=-1)

def to_chunks(x, L):
    B, T, H = x.shape[:3]
    x = x.reshape((B, T // L, L, H) + x.shape[3:])
    return jnp.moveaxis(x, (1, 2), (0, 3))

def from_chunks(x):
    x = jnp.moveaxis(x, (0, 3), (1, 2))
    B, NC, L, H = x.shape[:4]
    return x.reshape((B, NC * L, H) + x.shape[4:])

def retention(q, k, v, S0, log_gamma):
    T = q.shape[1]
    L = min(CHUNK, T)
    idx = jnp.arange(L, dtype=jnp.float32)
    rel = idx[:, None] - idx[None, :]
    decay = jnp.where(rel >= 0, jnp.exp(log_gamma[:, None, None] * jnp.maximum(rel, 0.0)), 0.0)
    q_decay = jnp.exp(log_gamma[:, None] * (idx + 1.0))[..., None]
    k_decay = jnp.exp(log_gamma[:, None] * (L - 1.0 - idx))[..., None]
    chunk_decay = jnp.exp(log_gamma * L)[:, None, None]

    def step(S, inp):
        qc, kc, vc = inp
        scores = jnp.einsum('bhid,bhjd->bhij', qc, kc) * decay
        out = jnp.einsum('bhij,bhje->bhie', scores, vc) + jnp.einsum('bhid,bhde->bhie', qc * q_decay, S)
        S = chunk_decay * S + jnp.einsum('bhjd,bhje->bhde', kc * k_decay, vc)
        return S, out

    S, out = lax.scan(step, S0, (to_chunks(q, L), to_chunks(k, L), to_chunks(v, L)))
    return S, from_chunks(out)

def mlstm(q, k, v, i_pre, log_f, C0, n0, m0):
    T = q.shape[1]
    L = min(CHUNK, T)
    causal = jnp.tril(jnp.ones((L, L), dtype=bool))

    def step(carry, inp):
        C, n, m = carry
        qc, kc, vc, ic, fc = inp
        b = jnp.cumsum(fc, axis=-1)
        d_log = jnp.where(causal, b[..., :, None] - b[..., None, :] + ic[..., None, :], -jnp.inf)
        inter_log = b + m[..., None]
        m_t = jnp.maximum(inter_log, jnp.max(d_log, axis=-1))
        w_intra = jnp.exp(d_log - m_t[..., None])
        w_inter = jnp.exp(inter_log - m_t)
        s = jnp.einsum('bhid,bhjd->bhij', qc, kc) * w_intra
        num = jnp.einsum('bhij,bhje->bhie', s, vc) + w_inter[..., None] * jnp.einsum('bhid,bhde->bhie', qc, C)
        den = jnp.sum(s, axis=-1) + w_inter * jnp.einsum('bhid,bhd->bhi', qc, n)
        h = num / jnp.maximum(jnp.abs(den), jnp.exp(-m_t))[..., None]
        b_last = b[..., -1]
        w_log = b_last[..., None] - b + ic
        m_new = jnp.maximum(b_last + m, jnp.max(w_log, axis=-1))
        w_k = jnp.exp(w_log - m_new[..., None])[..., None] * kc
        carry_decay = jnp.exp(b_last + m - m_new)
        C = carry_decay[..., None, None] * C + jnp.einsum('bhjd,bhje->bhde', w_k, vc)
        n = carry_decay[..., None] * n + jnp.sum(w_k, axis=2)
        return (C, n, m_new), h

    inputs = (to_chunks(q, L), to_chunks(k, L), to_chunks(v, L), to_chunks(i_pre, L), to_chunks(log_f, L))
    (C, n, m), h = lax.scan(step, (C0, n0, m0), inputs)
    return C, n, m, from_chunks(h)

def causal_conv(x, buf, w, b):
    T = x.shape[1]
    xp = jnp.concatenate([buf.astype(x.dtype), x], axis=1)
    y = b
    for j in range(CONV_WIDTH):
        y = y + w[j] * xp[:, j:j + T]
    return jax.nn.silu(y), xp[:, xp.shape[1] - (CONV_WIDTH - 1):]

def moe(x, w_router, b_router, w_up, b_up, w_down, b_down):
    T, D = x.shape
    logits = (x @ w_router + b_router).astype(jnp.float32)
    top_vals, top_idx = lax.top_k(logits, TOP_K)
    gates = jax.nn.softmax(top_vals, axis=-1)
    flat_e = top_idx.reshape(-1)
    order = jnp.argsort(flat_e)
    sorted_e = flat_e[order]
    tok = order // TOP_K
    counts = jnp.bincount(flat_e, length=N_EXPERTS)
    padded = (counts + EXPERT_BLOCK - 1) // EXPERT_BLOCK * EXPERT_BLOCK
    pad_end = jnp.cumsum(padded)
    pad_start = pad_end - padded
    start = jnp.cumsum(counts) - counts
    dest = pad_start[sorted_e] + (jnp.arange(T * TOP_K) - start[sorted_e])
    n_blocks = -(-(T * TOP_K) // EXPERT_BLOCK) + N_EXPERTS
    cap = n_blocks * EXPERT_BLOCK
    slot_tok = jnp.full((cap,), T, dtype=jnp.int32).at[dest].set(tok.astype(jnp.int32))
    block_e = jnp.minimum(jnp.searchsorted(pad_end, jnp.arange(n_blocks) * EXPERT_BLOCK, side='right'), N_EXPERTS - 1)
    x_pad = jnp.concatenate([x, jnp.zeros((1, D), x.dtype)], axis=0)
    xb = x_pad[slot_tok].reshape(n_blocks, EXPERT_BLOCK, D)

    def expert(args):
        xe, e = args
        hu = xe @ w_up[e] + b_up[e]
        gate = jnp.minimum(hu[:, :D_FF], SWIGLU_LIMIT)
        lin = jnp.clip(hu[:, D_FF:], -SWIGLU_LIMIT, SWIGLU_LIMIT)
        glu = gate * jax.nn.sigmoid(SWIGLU_ALPHA * gate)
        return ((lin + 1.0) * glu) @ w_down[e] + b_down[e]

    yb = lax.map(expert, (xb, block_e))
    y_sorted = yb.reshape(cap, D)[dest]
    weights = gates.reshape(-1)[order]
    out = jax.ops.segment_sum(y_sorted.astype(jnp.float32) * weights[:, None], tok, num_segments=T)
    return out.astype(x.dtype)

def layer(x, pos, c, S_ret, C, n, m, conv_buf, w_mod, b_mod, g_mix, g_ffn, w_in, b_igate, b_fgate, w_conv, b_conv, g_ret, g_mlstm, w_out, w_router, b_router, w_up, b_up, w_down, b_down):
    B, T, D = x.shape
    f32 = jnp.float32
    mod = (jax.nn.silu(c) @ w_mod + b_mod)[:, None, :]
    sh_a, sc_a, gt_a, sh_f, sc_f, gt_f = jnp.split(mod, N_MOD, axis=-1)
    h = rms_norm(x, g_mix) * (1.0 + sc_a) + sh_a
    p = h @ w_in
    cuts = [int(s) for s in np.cumsum(PROJ_SIZES)[:-1]]
    rq, rk, rv, rg, mqk, mv, mo, mi, mf = jnp.split(p, cuts, axis=-1)

    def heads(t, H):
        return t.astype(f32).reshape(B, T, H, -1)

    log_gamma = jnp.log1p(-jnp.exp2(-5.0 - jnp.arange(RET_HEADS, dtype=f32)))
    q_r = rotary(heads(rq, RET_HEADS), pos)
    k_r = rotary(heads(rk, RET_HEADS), pos) * RET_HEAD_DIM ** -0.5
    S_new, y_r = retention(q_r, k_r, heads(rv, RET_HEADS), S_ret.astype(f32), log_gamma)
    y_r = jax.nn.silu(rg.astype(f32)) * head_norm(y_r, g_ret).reshape(B, T, RET_WIDTH)

    qk, conv_new = causal_conv(mqk, conv_buf, w_conv, b_conv)
    mq, mk = jnp.split(qk, 2, axis=-1)
    i_pre = mi.astype(f32) + b_igate.astype(f32)
    log_f = jax.nn.log_sigmoid(mf.astype(f32) + b_fgate.astype(f32))
    C_new, n_new, m_new, y_m = mlstm(heads(mq, MLSTM_HEADS), heads(mk, MLSTM_HEADS) * MLSTM_HEAD_DIM ** -0.5, heads(mv, MLSTM_HEADS), i_pre, log_f, C.astype(f32), n.astype(f32), m.astype(f32))
    y_m = jax.nn.sigmoid(mo.astype(f32)) * head_norm(y_m, g_mlstm).reshape(B, T, MLSTM_WIDTH)

    mixed = jnp.concatenate([y_r, y_m], axis=-1).astype(x.dtype) @ w_out
    x = x + gt_a * mixed
    h2 = rms_norm(x, g_ffn) * (1.0 + sc_f) + sh_f
    x = x + gt_f * moe(h2.reshape(B * T, D), w_router, b_router, w_up, b_up, w_down, b_down).reshape(B, T, D)
    return x, S_new, C_new, n_new, m_new, conv_new

def setup_inputs(seed: int = 0) -> dict:
    key = jax.random.key(seed)
    ks = iter(jax.random.split(key, 32))
    f32 = jnp.float32

    def nrm(shape, scale):
        return jax.random.normal(next(ks), shape, f32) * scale

    return {
        'x_prompt': nrm((BATCH, SEQ, D_MODEL), 1.0),
        'x_sample': nrm((DEC_BATCH, DEC_SEQ, D_MODEL), 1.0),
        'c_prompt': nrm((BATCH, D_MODEL), 1.0),
        'c_sample': nrm((DEC_BATCH, D_MODEL), 1.0),
        'state_ret': nrm((DEPTH, DEC_BATCH, RET_HEADS, RET_HEAD_DIM, RET_HEAD_DIM), 0.5),
        'state_mlstm_c': nrm((DEPTH, DEC_BATCH, MLSTM_HEADS, MLSTM_HEAD_DIM, MLSTM_HEAD_DIM), 0.5),
        'state_mlstm_n': nrm((DEPTH, DEC_BATCH, MLSTM_HEADS, MLSTM_HEAD_DIM), 0.5),
        'state_mlstm_m': nrm((DEPTH, DEC_BATCH, MLSTM_HEADS), 1.0),
        'state_conv': nrm((DEPTH, DEC_BATCH, CONV_WIDTH - 1, 2 * MLSTM_WIDTH), 1.0),
        'w_mod': nrm((DEPTH, D_MODEL, N_MOD * D_MODEL), 0.5 * D_MODEL ** -0.5),
        'b_mod': nrm((DEPTH, N_MOD * D_MODEL), 0.02),
        'g_mix': 1.0 + nrm((DEPTH, D_MODEL), 0.02),
        'g_ffn': 1.0 + nrm((DEPTH, D_MODEL), 0.02),
        'w_in': nrm((DEPTH, D_MODEL, PROJ_COLS), D_MODEL ** -0.5),
        'b_igate': nrm((DEPTH, MLSTM_HEADS), 0.1),
        'b_fgate': jnp.linspace(3.0, 6.0, MLSTM_HEADS, dtype=f32)[None, :] + nrm((DEPTH, MLSTM_HEADS), 0.1),
        'w_conv': nrm((DEPTH, CONV_WIDTH, 2 * MLSTM_WIDTH), CONV_WIDTH ** -0.5),
        'b_conv': nrm((DEPTH, 2 * MLSTM_WIDTH), 0.02),
        'g_ret': 1.0 + nrm((DEPTH, RET_HEADS, RET_HEAD_DIM), 0.02),
        'g_mlstm': 1.0 + nrm((DEPTH, MLSTM_HEADS, MLSTM_HEAD_DIM), 0.02),
        'w_out': nrm((DEPTH, MIX_WIDTH, D_MODEL), MIX_WIDTH ** -0.5),
        'w_router': nrm((DEPTH, D_MODEL, N_EXPERTS), D_MODEL ** -0.5),
        'b_router': nrm((DEPTH, N_EXPERTS), 0.01),
        'w_up': nrm((DEPTH, N_EXPERTS, D_MODEL, 2 * D_FF), D_MODEL ** -0.5),
        'b_up': nrm((DEPTH, N_EXPERTS, 2 * D_FF), 0.02),
        'w_down': nrm((DEPTH, N_EXPERTS, D_FF, D_MODEL), D_FF ** -0.5),
        'b_down': nrm((DEPTH, N_EXPERTS, D_MODEL), 0.02),
        'g_final': 1.0 + nrm((D_MODEL,), 0.02),
    }

def reference(x_prompt, x_sample, c_prompt, c_sample, state_ret, state_mlstm_c, state_mlstm_n, state_mlstm_m, state_conv, w_mod, b_mod, g_mix, g_ffn, w_in, b_igate, b_fgate, w_conv, b_conv, g_ret, g_mlstm, w_out, w_router, b_router, w_up, b_up, w_down, b_down, g_final):
    f32 = jnp.float32
    bp, tp = x_prompt.shape[0], x_prompt.shape[1]
    ts = x_sample.shape[1]
    pos_p = jnp.arange(tp, dtype=jnp.int32)
    pos_s = PAST_LEN + jnp.arange(ts, dtype=jnp.int32)
    zero_ret = jnp.zeros((bp, RET_HEADS, RET_HEAD_DIM, RET_HEAD_DIM), f32)
    zero_c = jnp.zeros((bp, MLSTM_HEADS, MLSTM_HEAD_DIM, MLSTM_HEAD_DIM), f32)
    zero_n = jnp.zeros((bp, MLSTM_HEADS, MLSTM_HEAD_DIM), f32)
    zero_m = jnp.zeros((bp, MLSTM_HEADS), f32)
    zero_conv = jnp.zeros((bp, CONV_WIDTH - 1, 2 * MLSTM_WIDTH), x_prompt.dtype)
    xp, xs = x_prompt, x_sample
    new_p, new_s = [], []
    for l in range(DEPTH):
        lp = (w_mod[l], b_mod[l], g_mix[l], g_ffn[l], w_in[l], b_igate[l], b_fgate[l], w_conv[l], b_conv[l], g_ret[l], g_mlstm[l], w_out[l], w_router[l], b_router[l], w_up[l], b_up[l], w_down[l], b_down[l])
        xp, *st_p = layer(xp, pos_p, c_prompt, zero_ret, zero_c, zero_n, zero_m, zero_conv, *lp)
        xs, *st_s = layer(xs, pos_s, c_sample, state_ret[l], state_mlstm_c[l], state_mlstm_n[l], state_mlstm_m[l], state_conv[l], *lp)
        new_p.append(st_p)
        new_s.append(st_s)

    def stack(states, i):
        return jnp.stack([s[i] for s in states], axis=0)

    y_prompt = rms_norm(xp, g_final)
    y_sample = rms_norm(xs, g_final)
    return (y_prompt, y_sample, stack(new_p, 0), stack(new_p, 1), stack(new_p, 2), stack(new_p, 3), stack(new_p, 4), stack(new_s, 0), stack(new_s, 1), stack(new_s, 2), stack(new_s, 3), stack(new_s, 4))


_drawn_inputs = setup_inputs


def setup_inputs(seed=0):
    import zlib

    import numpy as np

    out = dict(_drawn_inputs(seed))
    spreads = {}
    factors = {'g_ffn': 3.414,
     'g_ret': 7.69,
     'g_mlstm': 8.0,
     'b_router': 5.831,
     'b_up': 8.0,
     'b_down': 33.583,
     'g_final': 9.349}
    for name, (base, spread) in spreads.items():
        noise = np.random.default_rng([zlib.crc32(name.encode()), seed]).standard_normal(out[name].shape)
        drawn = base * np.exp(spread * noise) if base else spread * noise
        out[name] = __import__('jax').numpy.asarray(drawn.astype(out[name].dtype))
    for name, factor in factors.items():
        out[name] = (out[name] * factor).astype(out[name].dtype)
    return out
```

```python
import numpy as np
import concourse.bass as bass
from concourse import mybir
from contextlib import ExitStack

D = 1024
KD = D // 128
SEQ, NSEQ, TS = 256, 8, 8
NTOK = SEQ + NSEQ * TS
NT = 3
ROWS = [128, 128, 64]
H = 4
HD = 128
NE = 32
EPS = 1e-6
SCALE = HD ** -0.5
NEG = -1e30
PAST = 2048
BIG_BLOCK = 128
SIZES = (32, 64, 128)
ROUNDS = -(-NTOK // BIG_BLOCK)
SLOT = 4096


def log_gamma():
    return np.log1p(-np.exp2(-5.0 - np.arange(H, dtype=np.float32))).astype(np.float32)


def constant_tables():
    f = np.float32
    i = np.arange(128)
    t = {}
    t["ident"] = np.eye(128, dtype=f)
    t["ones"] = np.ones((128, 128), f)
    low = i[None, :] <= i[:, None]
    same = (i[:, None] // TS) == (i[None, :] // TS)
    t["mask"] = np.where(low, 0, NEG).astype(f)
    t["maskT"] = np.ascontiguousarray(t["mask"].T)
    t["tri"] = low.T.astype(f)
    sm = np.where(low & same, 0, NEG).astype(f)
    t["maskS"] = sm[:, :64].copy()
    t["maskST"] = np.ascontiguousarray(sm.T)[:, :64].copy()
    t["triS"] = (low & same).T.astype(f)[:, :64].copy()
    lg = log_gamma()
    rel = (i[None, :] - i[:, None]).astype(f)
    dec = np.exp(lg[:, None, None] * np.maximum(rel, 0)) * (rel >= 0)
    t["decT"] = (dec * f(SCALE)).astype(f).transpose(1, 0, 2).reshape(128, H * 128)
    t["decTS"] = (dec * f(SCALE) * same).astype(f).transpose(1, 0, 2)[:, :, :64].reshape(128, H * 64)
    pos = np.stack([i, i + 128, PAST + i % TS], 1).astype(f)
    inv = np.power(f(10000.0), -np.arange(64, dtype=f) / f(64)).astype(f)
    ang = (pos[:, :, None] * inv).astype(f)
    t["cos"] = np.cos(ang).astype(f).reshape(128, NT * 64)
    t["sin"] = np.sin(ang).astype(f).reshape(128, NT * 64)
    idx = np.stack([i, i, i % TS], 1).astype(f)
    length = np.array([128, 128, TS], f)
    t["qdec"] = np.exp(lg * (idx[:, :, None] + 1)).astype(f).reshape(128, NT * H)
    t["kdec"] = (np.exp(lg * (length[None, :, None] - 1 - idx[:, :, None])) * f(SCALE)).astype(f).reshape(128, NT * H)
    t["seqmask"] = ((i[:, None] // TS) == np.arange(NSEQ)[None, :]).astype(f)
    t["slots"] = np.tile(np.arange(ROUNDS * 128, dtype=f), (128, 1))
    t["biasrow"] = ((i[:, None] % 32 == np.arange(33)[None, :] % NE) & (i[:, None] // 32 != 1)).astype(f)
    t["eidx"] = np.tile(np.arange(32, dtype=f), (128, 1))
    return {k: np.ascontiguousarray(v.astype(f)) for k, v in t.items()}


def gate_selectors():
    s = np.zeros((128, 4, NTOK), np.float32)
    cond = np.concatenate([np.zeros(SEQ, int), 1 + np.arange(NSEQ * TS) // TS])
    for t in range(4):
        s[32 * t + cond, t, np.arange(NTOK)] = 1
    return s.reshape(128, 4 * NTOK)


def build(nc, a):
    F32, BF, I32, U32 = mybir.dt.float32, mybir.dt.bfloat16, mybir.dt.int32, mybir.dt.uint32
    ALU, ACT, AX = mybir.AluOpType, mybir.ActivationFunctionType, mybir.AxisListType
    X = AX.X
    tabs = constant_tables()
    lg = log_gamma()
    ctx = ExitStack()
    with ctx:
        WORDS = 53100
        mem = ctx.enter_context(nc.sbuf_tensor("mem", [128, WORDS], F32))
        psum = ctx.enter_context(nc.psum_tensor("psum", [128, 8, 512], F32))

        def at(off, *shape):
            n = int(np.prod(shape))
            assert off + n <= WORDS, (off, shape)
            v = mem[:, off:off + n]
            if len(shape) == 1:
                return v
            names = "abcd"[:len(shape)]
            return v.rearrange(f"p ({' '.join(names)}) -> p {' '.join(names)}",
                               **{k: s for k, s in zip(names, shape)})

        def at_bf(off, *shape):
            n = int(np.prod(shape))
            v = mem[:, off:off + n // 2].bitcast(BF)
            if len(shape) == 1:
                return v
            names = "abcd"[:len(shape)]
            return v.rearrange(f"p ({' '.join(names)}) -> p {' '.join(names)}",
                               **{k: s for k, s in zip(names, shape)})

        def slot8(s):
            return at(s * SLOT, 8, 512)

        cursor = [6 * SLOT]

        def take(n):
            o = cursor[0]
            cursor[0] += n
            assert cursor[0] <= WORDS, cursor[0]
            return o

        const_off = {}
        C0 = cursor[0]
        for k, v in tabs.items():
            const_off[k] = take(v.shape[1])
        CW = cursor[0] - C0

        def K(name, *shape):
            v = tabs[name]
            return at(const_off[name], *(shape or (v.shape[1],)))

        ident = K("ident")
        ones = K("ones")
        cT = at(take(KD * 32), KD, 32)
        parT = at(take(KD * 32), KD, 32)
        coefA = at(take(KD * 9), KD, 9)
        coefF = at(take(KD * 9), KD, 9)
        stat = at(take(160), 160)
        gt = {k: at(take(NT * H), NT, H) for k in
              ("ipre", "fpre", "fabs", "b", "g", "M", "mt", "mprev", "wint", "expm", "wk", "btot", "mlast")}
        igf = at(take(16), 16)
        m0all = at(take(32), NSEQ, H)
        m0tok = at(take(4), 4)
        cdec = at(take(64), 2, 32)
        nT = at(take(64), 2, 32)
        wg = at(take(KD * 8), KD, 8)
        wr = at(take(KD * NE), KD, NE)
        pos = at(take(NT * 33), NT, 33)
        gate = at(take(NT * 33), NT, 33)
        route = at(take(NT * NE), NT, NE)
        brout = at(take(NE), NE)
        counts = at(take(33), 33)
        counts_i = mem[:, cursor[0]:cursor[0] + 33].bitcast(I32)
        take(33)
        hr = at(take(4), 4)
        mv2 = at(take(8), H, 2)
        top8 = at(take(24), NT, 8)
        idx8 = mem[:, cursor[0]:cursor[0] + 24].bitcast(U32).rearrange("p (t k) -> p t k", t=NT)
        take(24)
        idxf = at(take(24), NT, 8)
        nmax = at(take(4), 4)
        logit = at(take(96), NT, 32)
        pexp = at(take(96), NT, 32)
        ss = at(take(8), 8)
        halves = at(take(4), 4)
        rs = at(take(8), 8)
        B0 = cursor[0]

        o = B0
        hT = at(o, KD, NTOK)
        gnorm = at(o, 2, 512)
        comb = at(o + 1024, H, HD + 1)
        nrm = at(o + 1540, H, 128)
        xg = at(o, KD, 128)
        Pg = at(o + 1024, NT, 128); G = at(o + 1408, NTOK); P = at_bf(o + 1728, NT, 128)
        bsel = at_bf(o + 1920, 128)
        o += KD * NTOK
        modr = at(o, 12, 128)
        bparts = at_bf(o, 3 * D)
        o += 1536
        modT = at(o, 48, 9); o += 432
        o2 = o
        rk = at(o, NT, 512); rv = at(o + 1536, NT, 512); yfin = at(o, NT, D); prow = at(o + 1536, D)
        acc = yfin; o += 3072
        o3 = o
        mo = at(o, NT, 512); rg = at(o + 1536, NT, 512); xin = at(o, NT, D); gateA = xin
        h2p = at_bf(o, 3, NT, D); o += 3072
        o4 = o
        rq = at(o, NT, 512); crow = at(o, D); o += 1536
        gateF = at(o, NT, D)
        xpp = at(o, KD, 3 + SEQ); xps = at(o + KD * (3 + SEQ), KD, NSEQ, 3 + TS)
        o += KD * (3 + SEQ) + KD * NSEQ * (3 + TS)
        o5 = o
        qkT = at(o, KD, NTOK); o += KD * NTOK
        rT = at(o, KD, NTOK); xnT = rT; o += KD * NTOK
        x2 = at(o5 + 296, NT, D)
        sel = at(o5 + 3368, 4, NTOK)
        xnT2 = at(o5 + 4648, KD, NTOK); lgT = at(o5 + 4648, NTOK)
        gt_ = at(o5 + 3368, 2, 512); sg = at(o5 + 4392, 2, 512); li = at(o5 + 5416, 2, 512)
        actT = at(o5 + 6440, KD, 128); yd = at(o5 + 7464, 2, 512)
        gfin = li
        assert o5 + 7464 + 1024 <= WORDS, o5 + 8488
        vaug = at(o, NT, H, HD + 1); o += NT * H * (HD + 1)
        Wm = at(o, NT, H, 128); o += 1536
        tmpA = at(o, H, 128); o += 512
        assert o <= WORDS, o
        o = 4 * SLOT
        S0 = at(o, 2, NSEQ, HD + 1); bmod = at(o, 12, 128); o += 2 * NSEQ * (HD + 1)
        QM = at(o, 2, NSEQ, 72); QMF = at(o, 2, 576); o += 1152
        vmask = at(o, NSEQ, HD); convrow = at(o, D); lgTm = at(o, NTOK); o += 1024
        Cst = at(o, 2, H, HD + 1); o += 2 * H * (HD + 1)
        sT = at(o, H, 128); cbuf = at(o, KD, 27); o += 512
        tmpB = at(o, H, 128); o += 512
        km = at(o, NT, 512); o += 1536
        gtok = at(o, NT, 8); o += 24
        nrow = at(o, 128); o += 128
        mlS = at(o, H, NSEQ); o += 32
        assert o <= 6 * SLOT, o

        brows = at(o5 + 4392, 3 * D)
        SMALL, STORES = 14, 6

        def square_view(v, n):
            return v.rearrange("p h j -> p (h j)")[0:n, 0:H * n].rearrange("p (h j) -> p h j", h=H)

        def tmpA_v(n):
            return tmpA.rearrange("p h j -> p (h j)")[0:n, 0:H * n]

        sems = {}

        def S(name):
            if name not in sems:
                sems[name] = ctx.enter_context(nc.semaphore(name))
            return sems[name]

        loaded = [S(f"slot{c}_loaded") for c in range(6)]
        used = [S(f"slot{c}_used") for c in range(6)]

        def by_size(eng, count, f):
            if count is None:
                f(SIZES[2])
                return
            with eng.If(count <= SIZES[0]):
                f(SIZES[0])
            with eng.Else():
                with eng.If(count <= SIZES[1]):
                    f(SIZES[1])
                with eng.Else():
                    f(SIZES[2])

        def flat(bank0, n):
            return psum[:, bank0:bank0 + -(-n // 512), :].rearrange("p b n -> p (b n)")[:, 0:n]

        def chained(eng, name):
            n = [0]

            def step(ins):
                n[0] += 1
                ins.then_inc(S(name), 1)
                eng.wait_ge(S(name), n[0])
            return step

        COL = {"rq": 0, "rk": 512, "rv": 1024, "rg": 1536, "mqk0": 2048, "mqk1": 2560, "mv": 3072, "mo": 3584}
        CH = (["mod0", "mod1", "mod2", "mod3", "mqk0", "mod4", "mqk1", "mod5", "rq", "mod6", "rk", "mod7",
               "mv", "mod8", "rv", "mod9", "mo", "mod10", "rg", "mod11", "out0", "out1"])
        NCH = len(CH)
        USES = [len(range(c, NCH, 4)) if c < 4 else 0 for c in range(6)]

        def chunk_source(name):
            if name.startswith("mod"):
                w, c = a["w_mod"][0], 512 * int(name[3:])
            elif name.startswith("out"):
                w, c = a["w_out"][0], 512 * int(name[3:])
            else:
                w, c = a["w_in"][0], COL[name]
            return w[:, c:c + 512].rearrange("(k p) n -> p k n", p=128)

        OUTS = ["c", "par", "nstate"] + [f"mod{n}" for n in range(4)] + [f"modT{n}" for n in range(4)]
        OUTS += [f"xnT{k}" for k in range(KD)]
        for n in range(4, 20):
            c = CH[n]
            if c.startswith("mod"):
                OUTS.append(c)
            elif c.startswith("mqk"):
                OUTS += [f"{c}_{m}" for m in range(4)]
                if c == "mqk1":
                    OUTS += ["gates", "gatesT"]
            else:
                OUTS += [f"{c}_{t}" for t in range(NT)]
                if c == "mv":
                    OUTS += [f"km{t}" for t in range(NT)] + ["conv0", "conv1"]
                if c == "rv":
                    OUTS += [f"rT{h}" for h in range(2 * H)]
        OUTS += [f"modT{n}" for n in (6, 7, 8, 9)]
        Q = {n: q for q, n in enumerate(OUTS)}
        NQ = len(OUTS)
        GROUPS = [(0, 0), (1, 0), (0, 1), (1, 1), (0, 2), (1, 2)]

        def tok(t):
            return slice(128 * t, 128 * t + ROWS[t])

        block = ctx.enter_context(nc.Block())

        @block.sync
        def _(sp):
            sp.dma_start(crow[0:1, :], a["c_prompt"]).then_inc(S("c_in"), 16)
            sp.dma_start(crow[1:9, :], a["c_sample"]).then_inc(S("c_in"), 16)
            sp.dma_start(at(C0, CW), a["tables"]).then_inc(S("tables_in"), 16)
            for n in range(2):
                sp.dma_start(slot8(n), chunk_source(CH[n])).then_inc(loaded[n], 16)
            sp.dma_start(xin[:, 0:2, :], a["x_prompt"][0].rearrange("(t p) d -> p t d", p=128)).then_inc(S("x_in"), 16)
            sp.dma_start(xin[0:64, 2, :], a["x_sample"].rearrange("b t d -> (b t) d")).then_inc(S("x_in"), 16)
            for n in range(2, NCH):
                if n >= 4:
                    sp.wait_ge(used[n % 4], n // 4)
                sp.dma_start(slot8(n % 4), chunk_source(CH[n])).then_inc(loaded[n % 4], 16)

            def expert_chunk(e, c):
                if c < 4:
                    src = a["w_up"][0][e, 256 * c:256 * (c + 1), :].rearrange("(j p) n -> p j n", p=128)
                    dst = at(c * SLOT, 2, 2 * D)
                else:
                    src = a["w_down"][0][e, 512 * (c - 4):512 * (c - 3), :].rearrange("(j p) n -> p j n", p=128)
                    dst = at(c * SLOT, 4, D)
                sp.dma_start(dst, src).then_inc(loaded[c], 16)

            for c in (2, 3, 4, 5, 0, 1):
                if c < 4:
                    sp.wait_ge(used[c], USES[c])
                elif c == 4:
                    sp.wait_ge(S("y_ready"), len(GROUPS))
                    sp.wait_ge(S("state_out"), 16 * STORES)
                    for u in range(2):
                        sp.wait_ge(S(f"S0_out{u}"), 16 * H)
                expert_chunk(0, c)
            with sp.Fori(1, NE) as e:
                for c in range(6):
                    sp.wait_ge(used[c], e + USES[c])
                    expert_chunk(e, c)
            sp.wait_ge(S("counts_ready"), 1)
            most = sp.value_load(counts_i[0:1, NE:NE + 1], min_val=0, max_val=NTOK)
            with sp.If(most > BIG_BLOCK):
                with sp.Fori(1, ROUNDS) as r:
                    with sp.Fori(0, NE) as e:
                        for c in range(6):
                            sp.wait_ge(used[c], r * NE + e + USES[c])
                            expert_chunk(e, c)
            with sp.Else():
                sp.nop()
            sp.wait_ge(S("y_out"), 16 * 2)
            sp.wait_ge(S("state_out"), 16 * STORES)

        @block.tensor
        def _(pe):
            chunk_n = [0]

            def bank_free(q):
                if q >= 8:
                    pe.wait_ge(S("evacuated"), q - 7)

            def take_chunk(n):
                pe.wait_ge(loaded[n % 4], 16 * (n // 4 + 1))
                return slot8(n % 4)

            pe.wait_ge(S("tables_in"), 16)
            pe.wait_ge(S("c_silu"), 1)
            for k in range(KD):
                last = pe.transpose(psum[:, 0, 32 * k:32 * k + 9], crow[0:9, 128 * k:128 * k + 128], ident[0:9, 0:9])
            last.then_inc(S("projected"), 1)
            pe.wait_ge(S("params_in"), 16 * 5)
            for k in range(KD):
                last = pe.transpose(psum[:, 1, 31 * k:31 * k + 31], prow[0:31, 128 * k:128 * k + 128], ident[0:31, 0:31])
            last.then_inc(S("projected"), 1)
            pe.wait_ge(S("nstate_in"), 16)
            pe.transpose(psum[:, 2, 0:32], nrow[0:32, :], ident[0:32, 0:32]).then_inc(S("projected"), 1)

            def mod_rows(name, n):
                q = Q[name]
                w = take_chunk(n)
                bank_free(q)
                for k in range(KD):
                    for t in range(4):
                        last = pe.matmul(psum[32 * t:32 * t + 32, q % 8, 0:128], cT[:, k, :],
                                         w[:, k, 128 * t:128 * t + 128], start=(k == 0), stop=(k == KD - 1))
                last.then_inc(used[n % 4], 1)
                pe.wait_ge(used[n % 4], n // 4 + 1)
                pe.nop().then_inc(S("projected"), 1)

            def mod_transposed(n):
                q = Q[f"modT{n}"]
                bank_free(q)
                pe.wait_ge(S("mod_biased"), MODB.index(n) + 1)
                pe.transpose(psum[:, q % 8, 0:128], modr[:, n, :], ident).then_inc(S("projected"), 1)

            MODB = list(range(12))
            pe.wait_ge(S("evacuated"), 1)
            for n in range(4):
                mod_rows(f"mod{n}", n)
            for n in range(4):
                mod_transposed(n)
            pe.wait_ge(S("xn_ready"), 3)
            for k in range(KD):
                q = Q[f"xnT{k}"]
                bank_free(q)
                for t in range(NT):
                    last = pe.transpose(psum[:, q % 8, tok(t)], xin[0:ROWS[t], t, 128 * k:128 * k + 128],
                                        ident[0:ROWS[t], 0:ROWS[t]])
                last.then_inc(S("projected"), 1)
            pe.wait_ge(S("h_ready"), 1)
            for n in range(4, 20):
                name = CH[n]
                if name.startswith("mod"):
                    mod_rows(name, n)
                    continue
                w = take_chunk(n)
                if name.startswith("mqk"):
                    for m in range(4):
                        q = Q[f"{name}_{m}"]
                        bank_free(q)
                        for k in range(KD):
                            last = pe.matmul(psum[:, q % 8, 0:NTOK], w[:, k, 128 * m:128 * m + 128], hT[:, k, :],
                                             start=(k == 0), stop=(k == KD - 1))
                        if m == 3:
                            last.then_inc(used[n % 4], 1)
                            pe.wait_ge(used[n % 4], n // 4 + 1)
                            pe.nop().then_inc(S("projected"), 1)
                        else:
                            last.then_inc(S("projected"), 1)
                else:
                    for t in range(NT):
                        q = Q[f"{name}_{t}"]
                        bank_free(q)
                        for k in range(KD):
                            if t < 2:
                                last = pe.matmul(psum[:, q % 8, :], hT[:, k, tok(t)], w[:, k, :],
                                                 start=(k == 0), stop=(k == KD - 1))
                            else:
                                for u in range(2):
                                    last = pe.matmul(psum[64 * u:64 * u + 64, q % 8, 0:256], hT[:, k, tok(t)],
                                                     w[:, k, 256 * u:256 * u + 256], start=(k == 0),
                                                     stop=(k == KD - 1))
                        if t == 2:
                            last.then_inc(used[n % 4], 1)
                            pe.wait_ge(used[n % 4], n // 4 + 1)
                            pe.nop().then_inc(S("projected"), 1)
                        else:
                            last.then_inc(S("projected"), 1)
                if name == "mqk1":
                    q = Q["gates"]
                    bank_free(q)
                    pe.wait_ge(S("small_in"), 16 * SMALL)
                    for k in range(KD):
                        last = pe.matmul(psum[0:8, q % 8, 0:NTOK], wg[:, k, :], hT[:, k, :],
                                         start=(k == 0), stop=(k == KD - 1))
                    last.then_inc(S("projected"), 1)
                    q = Q["gatesT"]
                    bank_free(q)
                    pe.wait_ge(S("evacuated"), Q["gates"] + 1)
                    for t in range(NT):
                        last = pe.transpose(psum[0:ROWS[t], q % 8, 8 * t:8 * t + 8], lgTm[0:8, tok(t)], ident[0:8, 0:8])
                    last.then_inc(S("projected"), 1)
                if name == "mv":
                    pe.wait_ge(S("qk_ready"), 1)
                    for t in range(NT):
                        q = Q[f"km{t}"]
                        bank_free(q)
                        for h in range(H):
                            last = pe.transpose(psum[0:ROWS[t], q % 8, 128 * h:128 * h + 128],
                                                qkT[:, H + h, tok(t)], ident)
                        last.then_inc(S("projected"), 1)
                    pe.wait_ge(S("cbuf_ready"), 1)
                    for u in range(2):
                        q = Q[f"conv{u}"]
                        bank_free(q)
                        for k in range(4):
                            last = pe.transpose(psum[0:27, q % 8, 128 * k:128 * k + 128], cbuf[:, 4 * u + k, :], ident)
                        last.then_inc(S("projected"), 1)
                if name == "rv":
                    for h in range(2 * H):
                        src = (rq, rk)[h // H]
                        pe.wait_ge(S("rotated"), h // H + 1)
                        q = Q[f"rT{h}"]
                        bank_free(q)
                        for t in range(NT):
                            last = pe.transpose(psum[:, q % 8, tok(t)],
                                                src[0:ROWS[t], t, 128 * (h % H):128 * (h % H) + 128],
                                                ident[0:ROWS[t], 0:ROWS[t]])
                        last.then_inc(S("projected"), 1)
            for n in (6, 7, 8, 9):
                mod_transposed(n)
            pe.wait_ge(S("evacuated"), NQ)

            pe.wait_ge(S("logf_ready"), 1)
            for t in range(NT):
                n = ROWS[t]
                tri = K("tri") if t < 2 else K("triS")
                pe.matmul(psum[0:n, 0, 4 * t:4 * t + 4], tri[0:n, 0:n], gt["fpre"][0:n, t, :], start=True, stop=True)
            for t in range(2):
                last = pe.matmul(psum[:, 0, 12 + 4 * t:16 + 4 * t], ones, gt["fpre"][:, t, :], start=True, stop=True)
            last.then_inc(S("cumsum_done"), 1)
            for t in range(NT):
                n = ROWS[t]
                pe.wait_ge(S("diag_ready"), 2 * t + 1)
                pe.matmul(psum[0:n, 1, 0:H * n], ones[0:n, 0:n], tmpA_v(n), start=True, stop=True).then_inc(S("spread"), 1)
                pe.wait_ge(S("diag_ready"), 2 * t + 2)
                pe.matmul(psum[:, 2, 0:H * n], ones[0:n, :], tmpA_v(n), start=True, stop=True).then_inc(S("spread"), 1)

            def score_bank(g):
                return 0 if g % 2 == 0 else 7

            def scores(g):
                kind, t = GROUPS[g]
                n = ROWS[t]
                src = qkT if kind else rT
                if g >= 2:
                    pe.wait_ge(S("sT_ready"), g - 1)
                for h in range(H):
                    last = pe.matmul(psum[0:n, score_bank(g), n * h:n * h + n], src[:, H + h, tok(t)],
                                     src[:, h, tok(t)], start=True, stop=True)
                last.then_inc(S("scored"), 1)

            scores(0)
            for g, (kind, t) in enumerate(GROUPS):
                n = ROWS[t]
                w = HD + kind
                src = qkT if kind else rT
                kt = km if kind else rk
                if g + 1 < len(GROUPS):
                    scores(g + 1)
                pe.wait_ge(S("sT_ready"), g + 1)
                pe.wait_ge(S("keys_ready"), 1 + kind)
                if g:
                    pe.wait_ge(S("combined"), g)
                for h in range(H):
                    v = vaug[0:n, t, h, :] if kind else rv[0:n, t, 128 * h:128 * h + 128]
                    last = pe.matmul(psum[0:n, 1 + h // 2, 129 * (h % 2):129 * (h % 2) + w], sT[0:n, h, 0:n], v,
                                     start=True, stop=True)
                last.then_inc(S("intra_done"), 1)
                if t < 2:
                    if t == 1:
                        pe.wait_ge(S("carried"), kind + 1)
                        for h in range(H):
                            last = pe.matmul(psum[0:n, 3 + h // 2, 129 * (h % 2):129 * (h % 2) + w],
                                             src[:, h, tok(t)], Cst[:, kind, h, 0:w], start=True, stop=True)
                        last.then_inc(S("inter_done"), 1)
                    if g:
                        pe.wait_ge(S("carried"), g)
                    for h in range(H):
                        v = vaug[0:n, t, h, :] if kind else rv[0:n, t, 128 * h:128 * h + 128]
                        last = pe.matmul(psum[:, 5 + h // 2, 129 * (h % 2):129 * (h % 2) + w],
                                         kt[0:n, t, 128 * h:128 * h + 128], v, start=True, stop=True)
                    last.then_inc(S("state_done"), 1)
                else:
                    for h in range(H):
                        i = kind * H + h
                        pe.wait_ge(S(f"S0_in{i % 2}"), 16 * (i // 2 + 1))
                        if kind:
                            pe.wait_ge(S("ncol_ready"), h + 1)
                        pe.wait_ge(S("qmask_ready"), i + 1)
                        for b in range(NSEQ):
                            last = pe.matmul(psum[0:64, 3 + h // 2, 129 * (h % 2):129 * (h % 2) + w],
                                             QMF[:, i % 2, 64 * b:64 * b + 64], S0[:, i % 2, b, 0:w],
                                             start=(b == 0), stop=(b == NSEQ - 1))
                        last.then_inc(S("inter_done"), 1)
                        pe.wait_ge(S("vmask_ready"), i + 1)
                        if i == 0:
                            pe.wait_ge(S("carried"), 4)
                        else:
                            pe.wait_ge(S("carriedS"), i)
                        for u in range(2):
                            last = pe.matmul(psum[:, 5 + u, :], kt[0:64, 2, 128 * h:128 * h + 128],
                                             vmask[0:64, 4 * u:4 * u + 4, :].rearrange("p b e -> p (b e)"),
                                             start=True, stop=True)
                        if kind:
                            last = pe.matmul(psum[:, 0, NSEQ * h:NSEQ * h + NSEQ], km[0:64, 2, 128 * h:128 * h + 128],
                                             K("seqmask")[0:64, :], start=True, stop=True)
                        last.then_inc(S("stateS_done"), 1)
            pe.wait_ge(S("carriedS"), 2 * H)
            pe.transpose(psum[0:32, 0, 0:128], nT[:, 1, :], ident)
            pe.transpose(psum[0:4, 0, 128:256], Cst[:, 1, :, HD], ident).then_inc(S("n_rows"), 1)

            pe.wait_ge(S("y_ready"), 6)
            for k in range(KD):
                if k == 0:
                    pe.wait_ge(S("n_copied"), 1)
                if k >= 6:
                    pe.wait_ge(S("evac2"), k - 5)
                y = (rg, mo)[k // H]
                for t in range(NT):
                    last = pe.transpose(psum[:, k % 6, tok(t)], y[0:ROWS[t], t, 128 * (k % H):128 * (k % H) + 128],
                                        ident[0:ROWS[t], 0:ROWS[t]])
                last.then_inc(S("proj2"), 1)

            def gate_rows(i0, n0):
                i = i0
                for t in range(NT):
                    for n in range(2):
                        pe.wait_ge(S("evac2"), i - 5)
                        for u in range(4):
                            last = pe.matmul(psum[0:ROWS[t], i % 6, 128 * u:128 * u + 128], sel[:, u, tok(t)],
                                             modr[:, n0 + n, :], start=True, stop=True)
                        last.then_inc(S("proj2"), 1)
                        i += 1

            pe.wait_ge(S("sel_in"), 16)
            gate_rows(KD, 4)
            pe.wait_ge(S("evac2"), KD)
            for t in range(NT):
                for u in range(2):
                    i = 2 * t + u
                    w = take_chunk(20 + u)
                    if i >= 2:
                        pe.wait_ge(S("residual"), i - 1)
                    for k in range(KD):
                        last = pe.matmul(psum[0:ROWS[t], 6 + u, :], hT[:, k, tok(t)], w[:, k, :],
                                         start=(k == 0), stop=(k == KD - 1))
                    last.then_inc(S("outproj"), 1)
            pe.wait_ge(S("outproj"), 6)
            pe.nop().then_inc(used[0], 1)
            pe.nop().then_inc(used[1], 1)
            gate_rows(KD + 6, 10)
            pe.wait_ge(S("xn2_ready"), 3)
            i = KD + 12
            for k in range(KD):
                pe.wait_ge(S("evac2"), i - 5)
                for t in range(NT):
                    last = pe.transpose(psum[:, i % 6, tok(t)], yfin[0:ROWS[t], t, 128 * k:128 * k + 128],
                                        ident[0:ROWS[t], 0:ROWS[t]])
                last.then_inc(S("proj2"), 1)
                i += 1
            pe.wait_ge(S("h2_ready"), 1)
            for k in range(KD):
                last = pe.matmul(psum[0:32, 6, 0:NTOK], wr[:, k, :], hT[:, k, :], start=(k == 0), stop=(k == KD - 1))
            last.then_inc(S("routerT"), 1)
            for t in range(NT):
                pe.wait_ge(S("evac2"), KD * 2 + 12)
                if t == 2:
                    pe.wait_ge(S("rest"), 1)
                for k in range(KD):
                    b = 2 * (t % 2) + k // 4
                    last = pe.transpose(psum[0:ROWS[t], b, 128 * (k % 4):128 * (k % 4) + 128], hT[:, k, tok(t)], ident)
                last.then_inc(S("h2_rows"), 1)
            pe.wait_ge(S("lgT_ready"), 1)
            for t in range(NT):
                last = pe.transpose(psum[0:ROWS[t], 7, 32 * t:32 * t + 32], lgT[0:32, tok(t)], ident[0:32, 0:32])
            last.then_inc(S("logits"), 1)
            pe.wait_ge(S("route_ready"), 1)
            for t in range(NT):
                n = ROWS[t]
                for s in range(t):
                    pe.matmul(psum[0:n, 6, 32 * t:32 * t + 32], ones[:, 0:n], route[:, s, :], start=(s == 0), stop=False)
                pe.matmul(psum[0:n, 6, 32 * t:32 * t + 32], K("tri")[0:n, 0:n], route[0:n, t, :],
                          start=(t == 0), stop=True)
            for s in range(NT):
                last = pe.matmul(psum[:, 6, 96:128], ones[0:ROWS[s], :], route[0:ROWS[s], s, :], start=(s == 0),
                                 stop=(s == NT - 1))
            last.then_inc(S("places"), 1)

            def gather(i, count):
                def products(slots):
                    pe.wait_ge(S("P_ready"), i + 1)
                    for k in range(KD):
                        for part in range(3):
                            for t in range(NT):
                                last = pe.matmul(psum[:, 4 + k // 4, 128 * (k % 4):128 * (k % 4) + slots],
                                                 h2p[:, part, t, 128 * k:128 * k + 128], P[:, t, 0:slots],
                                                 start=(part == 0 and t == 0), stop=(part == 2 and t == NT - 1))
                    last.then_inc(S("gathered"), 1)
                by_size(pe, count, products)

            def up_products(slots, weights):
                if slots == 32:
                    w = weights.rearrange("p (l n) -> p l n", l=2)
                    return [(psum[32 * q:32 * q + 32, 0, :], w[:, :, 256 * q:256 * q + 256]) for q in range(4)]
                if slots == 64:
                    return [(psum[64 * q:64 * q + 64, lin, :], weights[:, D * lin + 512 * q:D * lin + 512 * q + 512])
                            for lin in range(2) for q in range(2)]
                return [(psum[:, b, :], weights[:, 512 * b:512 * b + 512]) for b in range(4)]

            def up(it, slots):
                for c in range(4):
                    pe.wait_ge(loaded[c], 16 * (it + USES[c] + 1))
                    w = at(c * SLOT, 2, 2 * D)
                    for j in range(2):
                        for out, moving in up_products(slots, w[:, j, :]):
                            last = pe.matmul(out, xg[:, 2 * c + j, 0:slots], moving,
                                             start=(c == 0 and j == 0), stop=False)
                    last.then_inc(used[c], 1)
                for out, moving in up_products(slots, bparts[:, 0:2 * D]):
                    last = pe.matmul(out, bsel[:, 0:slots], moving, start=False, stop=True)
                last.then_inc(S("up_done"), 1)

            def turn_activations(it, slots):
                pe.wait_ge(S("act_ready"), it + 1)
                for j in range(KD * slots // 128):
                    last = pe.transpose(flat(0, D)[:, 128 * j:128 * j + 128],
                                        gt_.rearrange("p u n -> p (u n)")[:, 128 * j:128 * j + 128], ident)
                last.then_inc(S("act_turned"), 1)

            def down(it, slots):
                tiles = 128 // slots
                pieces = KD // tiles
                for u in range(2):
                    pe.matmul(psum[0:slots, 2 + u, :], bsel[:, 0:slots],
                              bparts[:, 2 * D + 512 * u:2 * D + 512 * u + 512], start=True, stop=False)
                pe.wait_ge(S("actT_ready"), it + 1)
                for c in (4, 5):
                    pe.wait_ge(loaded[c], 16 * (it + USES[c] + 1))
                last = [None, None]
                for j in range(pieces):
                    for u in range(2):
                        for q in range(tiles):
                            piece = q * pieces + j
                            c = piece // 4
                            last[c] = pe.matmul(psum[slots * q:slots * q + slots, 2 + u, :],
                                                actT[:, j, slots * q:slots * q + slots],
                                                at((4 + c) * SLOT, 4, D)[:, piece % 4, 512 * u:512 * u + 512],
                                                start=(j == 0 and q > 0), stop=(j == pieces - 1))
                last[0].then_inc(used[4], 1)
                last[1].then_inc(used[5], 1)

            def scatter(it, t):
                if t < 2:
                    for u in range(2):
                        last = pe.matmul(psum[:, 6 - 2 * t + u, :], G[:, tok(t)], yd[:, u, :], start=True, stop=True)
                else:
                    for u in range(2):
                        last = pe.matmul(psum[64 * u:64 * u + 64, 6, :], G[:, tok(t)], yd[:, u, :],
                                         start=True, stop=True)
                last.then_inc(S("scattered"), 1)

            def expert(r, e, it, count, count_next):
                ig = r * (NE + 1) + e
                pe.wait_ge(S("xg_ready"), ig + 1)
                pe.wait_ge(S("bsel_ready"), it + 1)
                pe.wait_ge(S("y_copied"), it + 1)
                by_size(pe, count, lambda slots: up(it, slots))
                gather(ig + 1, count_next)
                pe.wait_ge(S("G_ready"), it + 1)
                pe.wait_ge(S("added"), 3 * it + 1)
                scatter(it, 0)
                pe.wait_ge(S("xg_ready"), ig + 2)
                scatter(it, 1)
                by_size(pe, count, lambda slots: turn_activations(it, slots))
                pe.wait_ge(S("Pg_ready"), it + 1)
                pe.wait_ge(S("added"), 3 * it + 2)
                for t in range(NT):
                    n = ROWS[t]
                    last = pe.transpose(psum[:, 7, tok(t)], Pg[0:n, t, :], ident[0:n, 0:n])
                last.then_inc(S("Pg_turned"), 1)
                scatter(it, 2)
                pe.wait_ge(S("added"), 3 * it + 3)
                by_size(pe, count, lambda slots: down(it, slots))

            def last_scatter(its):
                pe.wait_ge(S("G_ready"), its + 1)
                pe.wait_ge(S("y_copied"), its + 1)
                pe.wait_ge(S("added"), 3 * its + 1)
                for t in range(NT):
                    if t == 2:
                        pe.wait_ge(S("added"), 3 * its + 2)
                    scatter(its, t)

            gather(0, None)
            with pe.Fori(0, NE) as e:
                count = pe.value_load(counts_i[0:1, bass.ds(e, 1)], min_val=0, max_val=NTOK)
                count_next = pe.value_load(counts_i[0:1, bass.ds(e + 1, 1)], min_val=0, max_val=NTOK)
                expert(0, e, e, count, count_next)
            most = pe.value_load(counts_i[0:1, NE:NE + 1], min_val=0, max_val=NTOK)
            with pe.If(most > BIG_BLOCK):
                with pe.Fori(1, ROUNDS) as r:
                    gather(r * (NE + 1), None)
                    with pe.Fori(0, NE) as e:
                        expert(r, e, r * NE + e, None, None)
                last_scatter(NE * ROUNDS)
            with pe.Else():
                last_scatter(NE)

        @block.scalar
        def _(act):
            for dst, src in ((prow[0:4, :], a["w_conv"][0]), (prow[4:5, :], a["b_conv"]),
                             (prow[5:6, :], a["g_mix"]), (prow[6:7, :], a["g_ffn"]),
                             (prow[7:31, :], a["state_conv"][0].rearrange("b j n -> (b j) n"))):
                act.dma_start(dst, src).then_inc(S("params_in"), 16)
            act.dma_start(nrow[0:32, :], a["state_mlstm_n"][0].rearrange("b h d -> (b h) d")).then_inc(S("nstate_in"), 16)
            for t in range(4):
                src = a["b_mod"][0].rearrange("(n t j) -> t n j", t=4, j=128)[t]
                act.dma_start(bmod[32 * t:32 * t + 32, :, :], src.partition_broadcast(32)).then_inc(S("bmod_in"), 16)
            act.dma_start(wg[:, :, :], a["w_in"][0][:, 4096:4104].rearrange("(k p) n -> p k n", p=128)).then_inc(S("small_in"), 16)
            act.dma_start(igf[:, 0:4], a["b_igate"][0].partition_broadcast(128)).then_inc(S("small_in"), 16)
            act.dma_start(igf[:, 4:8], a["b_fgate"][0].partition_broadcast(128)).then_inc(S("small_in"), 16)
            act.dma_start(wr[:, :, :], a["w_router"][0].rearrange("(k p) n -> p k n", p=128)).then_inc(S("small_in"), 16)
            act.dma_start(brout, a["b_router"][0].partition_broadcast(128)).then_inc(S("small_in"), 16)
            act.dma_start(m0all[:, :, :], a["state_mlstm_m"][0].partition_broadcast(128)).then_inc(S("small_in"), 16)
            for b in range(NSEQ):
                act.dma_start(m0tok[TS * b:TS * b + TS, :], a["state_mlstm_m"][0][b].partition_broadcast(TS)).then_inc(S("small_in"), 16)

            act.wait_ge(S("c_in"), 32)
            act.activation(crow[0:9, :], crow[0:9, :], ACT.Silu).then_inc(S("c_silu"), 1)

            def bank(q, n=128):
                return psum[0:n, q % 8, :]

            def evac(name, pairs):
                act.wait_ge(S("projected"), Q[name] + 1)
                for dst, src in pairs[:-1]:
                    act.copy(dst, src)
                act.copy(*pairs[-1]).then_inc(S("evacuated"), 1)

            def bq(name):
                return Q[name] % 8

            act.wait_ge(S("zeroed"), 1)
            evac("c", [(cT[:, :, 0:9], psum[:, 0, 0:256].rearrange("p (k c) -> p k c", k=KD)[:, :, 0:9])])
            evac("par", [(parT[:, :, 0:31], psum[:, 1, 0:248].rearrange("p (k c) -> p k c", k=KD))])
            evac("nstate", [(nT[:, 0, :], psum[:, 2, 0:32])])
            act.wait_ge(S("x_in"), 32)
            junk = at(o5, D)
            for t in range(NT):
                if t:
                    act.wait_ge(S("squares"), t)
                act.activation(junk[0:ROWS[t], :], xin[0:ROWS[t], t, :], ACT.Square,
                               accum_out=ss[0:ROWS[t], t:t + 1]).then_inc(S("squares"), 1)

            def evac_mod(n):
                evac(f"mod{n}", [(modr[:, n, :], psum[:, bq(f"mod{n}"), 0:128])])

            def evac_modT(n):
                src = psum[:, bq(f"modT{n}"), 0:128].rearrange("p (t c) -> p t c", t=4)[:, :, 0:9]
                evac(f"modT{n}", [(modT[:, 4 * n:4 * n + 4, :], src)])

            for n in range(4):
                evac_mod(n)
            for n in range(4):
                evac_modT(n)
            for k in range(KD):
                evac(f"xnT{k}", [(xnT[:, k, :], psum[:, bq(f"xnT{k}"), 0:NTOK])])
            DST = {"rq": rq, "rk": rk, "rv": rv, "rg": rg, "mo": mo}
            for n in range(4, 20):
                name = CH[n]
                if name.startswith("mod"):
                    evac_mod(int(name[3:]))
                elif name.startswith("mqk"):
                    for m in range(4):
                        k = 4 * int(name[3:]) + m
                        p = psum[:, bq(f"{name}_{m}"), :]
                        evac(f"{name}_{m}", [(xpp[:, k, 3:], p[:, 0:SEQ]),
                                             (xps[:, k, :, 3:], p[:, SEQ:NTOK].rearrange("p (b t) -> p b t", b=NSEQ))])
                else:
                    for t in range(NT):
                        b = bq(f"{name}_{t}")
                        if name == "mv":
                            def dst(n_, c0, c1):
                                return vaug[0:n_, t, c0 // 128:c1 // 128, 0:128]
                        else:
                            def dst(n_, c0, c1):
                                return DST[name][0:n_, t, c0:c1]
                        if t < 2:
                            src = psum[:, b, :]
                            if name == "mv":
                                src = src.rearrange("p (h e) -> p h e", h=4)
                            evac(f"{name}_{t}", [(dst(128, 0, 512), src)])
                        else:
                            pairs = []
                            for u in range(2):
                                src = psum[64 * u:64 * u + 64, b, 0:256]
                                if name == "mv":
                                    src = src.rearrange("p (h e) -> p h e", h=2)
                                pairs.append((dst(64, 256 * u, 256 * u + 256), src))
                            evac(f"{name}_{t}", pairs)
                if name == "mqk1":
                    evac("gates", [(lgTm[0:8, :], psum[0:8, bq("gates"), 0:NTOK])])
                    b = bq("gatesT")
                    evac("gatesT", [(gtok[:, 0:2, :], psum[:, b, 0:16].rearrange("p (t c) -> p t c", t=2)),
                                    (gtok[0:64, 2, :], psum[0:64, b, 16:24])])
                if name == "mv":
                    act.wait_ge(S("conv_done"), 1)
                    act.activation(qkT.rearrange("p k t -> p (k t)"), qkT.rearrange("p k t -> p (k t)"),
                                   ACT.Silu).then_inc(S("qk_ready"), 1)
                    for t in range(NT):
                        evac(f"km{t}", [(km[0:ROWS[t], t, :], bank(Q[f"km{t}"], ROWS[t]))])
                    for u in range(2):
                        evac(f"conv{u}", [(convrow[0:27, 512 * u:512 * u + 512], bank(Q[f"conv{u}"], 27))])
                    act.wait_ge(S("evacuated"), Q["conv1"] + 1)
                    act.dma_start(a["conv_p"][0, 0], convrow[0:3, :]).then_inc(S("conv_out"), 16)
                    act.dma_start(a["conv_s"][0].rearrange("b j n -> (b j) n"), convrow[3:27, :]).then_inc(S("conv_out"), 16)
                if name == "rv":
                    for h in range(2 * H):
                        evac(f"rT{h}", [(rT[:, h, :], psum[:, bq(f"rT{h}"), 0:NTOK])])
                if name == "mo":
                    act.wait_ge(S("evacuated"), Q["mo_2"] + 1)
                    for t in range(NT):
                        last = act.activation(mo[0:ROWS[t], t, :], mo[0:ROWS[t], t, :], ACT.Sigmoid)
                    last.then_inc(S("gate_act"), 1)
                if name == "rg":
                    act.wait_ge(S("evacuated"), Q["rg_2"] + 1)
                    for t in range(NT):
                        last = act.activation(rg[0:ROWS[t], t, :], rg[0:ROWS[t], t, :], ACT.Silu)
                    last.then_inc(S("gate_act"), 1)
            for n in (6, 7, 8, 9):
                evac_modT(n)

            act.wait_ge(S("fabs_ready"), 1)
            fa = gt["fabs"].rearrange("p t h -> p (t h)")
            act.activation(fa, fa, ACT.Exp, scale=-1.0).then_inc(S("fexp"), 1)
            act.wait_ge(S("fabs_ready"), 2)
            act.activation(fa, fa, ACT.Ln).then_inc(S("fexp"), 1)
            for t in range(NT):
                n = ROWS[t]
                act.wait_ge(S("W_in"), t + 1)
                tb = square_view(tmpB, n)
                for h in range(H):
                    last = act.activation(Wm[0:n, t, h, 0:n], tb[:, h, :], ACT.Exp, bias=gt["g"][0:n, t, h:h + 1])
                last.then_inc(S("W_done"), 1)
            act.wait_ge(S("exps_in"), 1)
            for v in (gt["wint"].rearrange("p t h -> p (t h)"), gt["expm"].rearrange("p t h -> p (t h)"),
                      cdec[:, 1, :]):
                act.activation(v, v, ACT.Exp)
            act.activation(cdec[:, 0, 0:4], cdec[:, 0, 0:4], ACT.Exp).then_inc(S("exps_done"), 1)
            act.dma_start(a["m_p"][0], gt["mt"][127:128, 1, :]).then_inc(S("state_out"), 16)
            act.dma_start(a["m_s"][0], gt["mt"][TS - 1:64:TS, 2, :]).then_inc(S("state_out"), 16)
            act.wait_ge(S("carried"), 3)
            act.dma_start(a["ret_p"][0, 0].rearrange("h d e -> d h e"), Cst[:, 0, :, 0:HD]).then_inc(S("state_out"), 16)
            act.wait_ge(S("carried"), 4)
            act.dma_start(a["c_p"][0, 0].rearrange("h d e -> d h e"), Cst[:, 1, :, 0:HD]).then_inc(S("state_out"), 16)
            for i in range(2 * H):
                act.wait_ge(S("carriedS"), i + 1)
                dst = a["c_s"] if i >= H else a["ret_s"]
                act.dma_start(dst[0][:, i % H].rearrange("b d e -> d b e"), S0[:, i % 2, :, 0:HD])\
                   .then_inc(S(f"S0_out{i % 2}"), 16)
            act.wait_ge(S("n_rows"), 1)
            act.copy(tmpB[0:32, 0, :], psum[0:32, 0, 0:128])
            act.copy(tmpB[0:4, 1, :], psum[0:4, 0, 128:256]).then_inc(S("n_copied"), 1)
            act.wait_ge(S("n_copied"), 1)
            act.dma_start(a["n_s"][0].rearrange("b h d -> (b h) d"), tmpB[0:32, 0, :]).then_inc(S("state_out"), 16)
            act.dma_start(a["n_p"][0, 0], tmpB[0:4, 1, :]).then_inc(S("state_out"), 16)
            act.wait_ge(S("stateS_done"), 8)
            act.wait_ge(S("qmask_ready"), 8)
            act.dma_start(x2[:, 0:2, :], a["x_prompt"][0].rearrange("(t p) d -> p t d", p=128)).then_inc(S("x2_in"), 16)
            act.dma_start(x2[0:64, 2, :], a["x_sample"].rearrange("b t d -> (b t) d")).then_inc(S("x2_in"), 16)
            act.dma_start(sel.rearrange("p u t -> p (u t)"), a["selectors"]).then_inc(S("sel_in"), 16)

            def evac2(i, dst, n, cols=512):
                act.wait_ge(S("proj2"), i + 1)
                act.copy(dst, psum[0:n, i % 6, 0:cols]).then_inc(S("evac2"), 1)

            for k in range(KD):
                evac2(k, hT[:, k, :], 128, NTOK)
            i = KD
            for t in range(NT):
                for u in range(2):
                    evac2(i, gateA[0:ROWS[t], t, 512 * u:512 * u + 512], ROWS[t])
                    i += 1
            for t in range(NT):
                act.wait_ge(S("residual"), 2 * t + 2)
                act.wait_ge(S("squares"), 3 + t)
                act.activation(yd.rearrange("p u n -> p (u n)")[0:ROWS[t], :], x2[0:ROWS[t], t, :], ACT.Square,
                               accum_out=ss[0:ROWS[t], 3 + t:4 + t]).then_inc(S("squares"), 1)
            for t in range(NT):
                for u in range(2):
                    evac2(i, gateF[0:ROWS[t], t, 512 * u:512 * u + 512], ROWS[t])
                    i += 1
            for k in range(KD):
                evac2(i, xnT2[:, k, :], 128, NTOK)
                i += 1
            act.wait_ge(S("routerT"), 1)
            act.copy(lgT[0:32, :], psum[0:32, 6, 0:NTOK]).then_inc(S("lgT_ready"), 1)
            for t in range(NT):
                n = ROWS[t]
                act.wait_ge(S("h2_rows"), t + 1)
                b = 2 * (t % 2)
                act.copy(h2p[0:n, 0, t, :], psum[0:n, b:b + 2, :].rearrange("p b n -> p (b n)")).then_inc(S("part"), 1)
                act.wait_ge(S("rest"), 2 * t + 1)
                act.copy(h2p[0:n, 1, t, :], yfin[0:n, t, :]).then_inc(S("part"), 1)
                act.wait_ge(S("rest"), 2 * t + 2)
                act.copy(h2p[0:n, 2, t, :], yfin[0:n, t, :]).then_inc(S("part"), 1)
            act.wait_ge(S("softmax_in"), 1)
            for t in range(NT):
                n = ROWS[t]
                last = act.activation(pexp[0:n, t, :], logit[0:n, t, :], ACT.Exp, bias=nmax[0:n, t:t + 1])
            last.then_inc(S("softmax_exp"), 1)

            def copy_gathered(i, count):
                def copy(slots):
                    act.wait_ge(S("gathered"), i + 1)
                    act.copy(xg[:, :, 0:slots], flat(4, D).rearrange("p (k s) -> p k s", k=KD)[:, :, 0:slots])\
                       .then_inc(S("xg_ready"), 1)
                by_size(act, count, copy)

            def expert(r, e, it, count, count_next):
                ig = r * (NE + 1) + e

                def sigmoid(slots):
                    n = 8 * slots
                    act.wait_ge(S("gate_ready"), it + 1)
                    act.activation(sg.rearrange("p u n -> p (u n)")[:, 0:n], gt_.rearrange("p u n -> p (u n)")[:, 0:n],
                                   ACT.Sigmoid, scale=1.702).then_inc(S("sig_ready"), 1)

                def turned(slots):
                    n = 8 * slots
                    act.wait_ge(S("act_turned"), it + 1)
                    act.copy(actT.rearrange("p j s -> p (j s)")[:, 0:n], flat(0, n)).then_inc(S("actT_ready"), 1)

                by_size(act, count, sigmoid)
                copy_gathered(ig + 1, count_next)
                by_size(act, count, turned)
                act.wait_ge(S("Pg_turned"), it + 1)
                act.wait_ge(S("scattered"), 3 * it + 3)
                act.copy(G, psum[:, 7, 0:NTOK]).then_inc(S("G_ready"), 1)
                act.wait_ge(used[4], it + 1)
                act.wait_ge(used[5], it + 1)
                act.copy(yd.rearrange("p u n -> p (u n)"), flat(2, D)).then_inc(S("y_copied"), 1)

            act.wait_ge(S("P_zero"), 1)
            act.nop().then_inc(S("G_ready"), 1)
            act.nop().then_inc(S("y_copied"), 1)
            copy_gathered(0, None)
            with act.Fori(0, NE) as e:
                count = act.value_load(counts_i[0:1, bass.ds(e, 1)], min_val=0, max_val=NTOK)
                count_next = act.value_load(counts_i[0:1, bass.ds(e + 1, 1)], min_val=0, max_val=NTOK)
                expert(0, e, e, count, count_next)
            most = act.value_load(counts_i[0:1, NE:NE + 1], min_val=0, max_val=NTOK)
            with act.If(most > BIG_BLOCK):
                with act.Fori(1, ROUNDS) as r:
                    copy_gathered(r * (NE + 1), None)
                    with act.Fori(0, NE) as e:
                        expert(r, e, r * NE + e, None, None)
            with act.Else():
                act.nop()
            act.wait_ge(S("moe_done"), 1)
            act.dma_start(gfin.rearrange("p u n -> p (u n)"), a["g_final"].partition_broadcast(128)).then_inc(S("gfin_in"), 16)
            for t in range(NT):
                act.wait_ge(S("x3_ready"), t + 1)
                act.wait_ge(S("squares"), 6 + t)
                act.activation(yd.rearrange("p u n -> p (u n)")[0:ROWS[t], :], x2[0:ROWS[t], t, :], ACT.Square,
                               accum_out=ss[0:ROWS[t], t:t + 1]).then_inc(S("squares"), 1)
            act.wait_ge(S("y_final"), 2)
            act.dma_start(a["y_prompt"][0].rearrange("(t p) d -> p t d", p=128), x2[:, 0:2, :]).then_inc(S("y_out"), 16)
            act.wait_ge(S("y_final"), 3)
            act.dma_start(a["y_sample"].rearrange("b t d -> (b t) d"), x2[0:64, 2, :]).then_inc(S("y_out"), 16)
            act.wait_ge(S("y_out"), 32)
            act.wait_ge(S("state_out"), 16 * STORES)
            act.wait_ge(S("conv_out"), 32)

        @block.gpsimd
        def _(pool):
            step = chained(pool, "pool_step")
            pool.memset(cT, 0.0)
            pool.memset(halves, -0.5)
            pool.memset(ss, 1.0)
            for k in gt:
                pool.memset(gt[k], 0.0)
            pool.memset(gtok, 0.0)
            pool.memset(QMF, 0.0)
            pool.memset(xpp[:, :, 0:3], 0.0)
            pool.memset(cdec, 0.0)
            pool.memset(vaug[:, :, :, HD:HD + 1], 1.0).then_inc(S("zeroed"), 1)
            pool.wait_ge(S("zeroed"), 1)

            def rstd(out, src, scale):
                step(pool.tensor_scalar(out, src, scale, EPS, ALU.mult, ALU.add))
                return pool.tensor_tensor(out, out, halves[0:out.shape[0], 0:out.shape[1]], ALU.pow)

            pool.wait_ge(S("squares"), 3)
            rstd(rs[:, 0:3], ss[:, 0:3], 1.0 / D).then_inc(S("rstd_ready"), 1)

            def mod_bias(n):
                pool.wait_ge(S("evacuated"), Q[f"mod{n}"] + 1)
                pool.tensor_tensor(modr[:, n, :], modr[:, n, :], bmod[:, n, :], ALU.add).then_inc(S("mod_biased"), 1)

            pool.wait_ge(S("bmod_in"), 64)
            for n in range(4):
                mod_bias(n)
            pool.wait_ge(S("evacuated"), Q["par"] + 1)
            for k in range(KD):
                last = pool.tensor_copy(xps[:, k, :, 0:3], parT[:, k, 7:31].rearrange("p (b j) -> p b j", b=NSEQ))
            last.then_inc(S("xps_ready"), 1)
            mod_bias(4)
            mod_bias(5)
            pool.wait_ge(S("evacuated"), Q["mqk1_3"] + 1)
            pool.wait_ge(S("xps_ready"), 1)
            pool.tensor_copy(cbuf[:, :, 0:3], xpp[:, :, SEQ:SEQ + 3])
            for k in range(KD):
                last = pool.tensor_copy(cbuf[:, k, 3:27].rearrange("p (b j) -> p b j", b=NSEQ), xps[:, k, :, TS:TS + 3])
            last.then_inc(S("cbuf_ready"), 1)
            for n in range(6, 12):
                mod_bias(n)
            pool.wait_ge(S("projected"), Q["rg_2"] + 1)
            pool.dma_start(gnorm[:, 0, :], a["g_ret"][0].rearrange("h d -> (h d)").partition_broadcast(128)).then_inc(S("gnorm_in"), 16)
            pool.dma_start(gnorm[:, 1, :], a["g_mlstm"][0].rearrange("h d -> (h d)").partition_broadcast(128)).then_inc(S("gnorm_in"), 16)

            def load_state(i):
                src = a["state_mlstm_c"] if i >= H else a["state_ret"]
                pool.dma_start(S0[:, i % 2, :, 0:HD], src[0][:, i % H].rearrange("b d e -> d b e"))\
                    .then_inc(S(f"S0_in{i % 2}"), 16)

            def mask_queries(i):
                q = (qkT if i >= H else rT)[:, i % H, SEQ:NTOK].rearrange("p (b t) -> p b t", b=NSEQ)
                pool.tensor_copy(QM[:, i % 2, :, 0:TS], q).then_inc(S("qmask_ready"), 1)

            def mask_values(i):
                h = i % H
                v = vaug[0:64, 2, h, 0:HD] if i >= H else rv[0:64, 2, 128 * h:128 * h + 128]
                pool.tensor_tensor(vmask[0:64, :, :], v.unsqueeze(1).to_broadcast([64, NSEQ, HD]),
                                   K("seqmask")[0:64, :].unsqueeze(2).to_broadcast([64, NSEQ, HD]),
                                   ALU.mult).then_inc(S("vmask_ready"), 1)

            pool.wait_ge(S("mod_biased"), 12)
            load_state(0)
            load_state(1)
            pool.wait_ge(S("gnorm_in"), 32)
            pool.wait_ge(S("gate_act"), 2)
            for t in range(NT):
                n = ROWS[t]
                pool.tensor_tensor(rg[0:n, t, :], rg[0:n, t, :], gnorm[0:n, 0, :], ALU.mult)
                last = pool.tensor_tensor(mo[0:n, t, :], mo[0:n, t, :], gnorm[0:n, 1, :], ALU.mult)
            last.then_inc(S("gates_scaled"), 1)
            pool.wait_ge(S("evacuated"), Q["rT7"] + 1)
            mask_queries(0)
            mask_queries(1)
            pool.wait_ge(S("conv_out"), 32)
            mask_values(0)

            def head_rstd(g):
                pool.wait_ge(S("moments"), g + 1)
                n = ROWS[GROUPS[g][1]]
                rstd(hr[0:n, :], mv2[0:n, :, 1], 1.0).then_inc(S("head_rstd"), 1)

            for g in range(4):
                head_rstd(g)
            for i in range(1, 2 * H):
                pool.wait_ge(S("stateS_done"), i)
                mask_values(i)
                if i >= 2:
                    mask_queries(i)
                    pool.wait_ge(S(f"S0_out{i % 2}"), 16 * (i // 2))
                    load_state(i)
                if i >= H:
                    pool.wait_ge(S(f"S0_in{i % 2}"), 16 * (i // 2 + 1))
                    pool.tensor_copy(S0[:, i % 2, :, HD:HD + 1],
                                     nT[:, 0, :].rearrange("p (b h) -> p b h", h=H)[:, :, i - H:i - H + 1])\
                        .then_inc(S("ncol_ready"), 1)
                if i == H:
                    head_rstd(4)
            head_rstd(5)
            pool.wait_ge(S("squares"), 6)
            rstd(rs[:, 0:3], ss[:, 3:6], 1.0 / D).then_inc(S("rstd_ready"), 1)
            pool.wait_ge(S("residual"), 6)
            pool.wait_ge(S("rstd_ready"), 2)
            step(pool.memset(h2p[64:128, :, 2, :], 0.0))
            pool.wait_ge(S("h2_ready"), 1)
            pool.wait_ge(S("h2_rows"), NT)
            pool.wait_ge(S("logits"), 1)
            pool.memset(G, 0.0)
            pool.memset(yd, 0.0)
            pool.memset(P, 0.0).then_inc(S("P_zero"), 1)
            pool.wait_ge(S("P_zero"), 1)
            for q in range(4):
                pool.dma_start(brows[32 * q:32 * q + 32, 0:2 * D], a["b_up"][0]).then_inc(S("brows_in"), 16)
                pool.dma_start(brows[32 * q:32 * q + 32, 2 * D:3 * D], a["b_down"][0]).then_inc(S("brows_in"), 16)
            pool.wait_ge(S("brows_in"), 16 * 8)
            step(pool.tensor_copy(bparts, brows))
            step(pool.tensor_tensor(brows[64:128, :], brows[64:128, :], bparts[64:128, :], ALU.subtract))
            step(pool.tensor_copy(bparts[64:128, :], brows[64:128, :]))
            step(pool.tensor_tensor(brows[96:128, :], brows[96:128, :], bparts[96:128, :], ALU.subtract))
            step(pool.tensor_copy(bparts[96:128, :], brows[96:128, :]))

            def expert(r, e, it):
                pool.wait_ge(used[4], it + 1)
                pick_bias(e + 1)

            def pick_bias(e):
                col = bass.ds(e, 1) if not isinstance(e, int) else slice(e, e + 1)
                pool.tensor_copy(bsel, K("biasrow")[:, col].to_broadcast([128, 128])).then_inc(S("bsel_ready"), 1)

            pick_bias(0)
            with pool.Fori(0, NE) as e:
                expert(0, e, e)
            pool.wait_ge(S("counts_ready"), 1)
            most = pool.value_load(counts_i[0:1, NE:NE + 1], min_val=0, max_val=NTOK)
            with pool.If(most > BIG_BLOCK):
                with pool.Fori(1, ROUNDS) as r:
                    with pool.Fori(0, NE) as e:
                        expert(r, e, r * NE + e)
            with pool.Else():
                pool.nop()
            for t in range(NT):
                pool.wait_ge(S("squares"), 7 + t)
                n = ROWS[t]
                rstd(rs[0:n, t:t + 1], ss[0:n, t:t + 1], 1.0 / D).then_inc(S("rstd3"), 1)

        @block.vector
        def _(dve):
            step = chained(dve, "dve_step")
            TT, TSC, STT = dve.tensor_tensor, dve.tensor_scalar, dve.scalar_tensor_tensor

            dve.wait_ge(S("rstd_ready"), 1)
            for t in range(NT):
                TSC(xin[0:ROWS[t], t, :], xin[0:ROWS[t], t, :], rs[0:ROWS[t], t:t + 1], None, ALU.mult)\
                    .then_inc(S("xn_ready"), 1)

            def modulate(src, coef, shift, n0, g_row, sem):
                step(STT(coef, modT[:, n0 + 8:n0 + 16, :], 1.0,
                         parT[:, :, g_row:g_row + 1].to_broadcast([128, KD, 9]), ALU.add, ALU.mult))
                for k in range(KD):
                    TSC(hT[:, k, 0:SEQ], src[:, k, 0:SEQ], coef[:, k, 0:1], modT[:, n0 + k, 0:1], ALU.mult, ALU.add)

                def seqs(v):
                    return v[:, :, SEQ:NTOK].rearrange("p k (b t) -> p k b t", b=NSEQ)

                def cols(v):
                    return v.unsqueeze(3).to_broadcast([128, KD, NSEQ, TS])
                step(TT(seqs(hT), seqs(src), cols(coef[:, :, 1:9]), ALU.mult))
                TT(seqs(hT), seqs(hT), cols(modT[:, n0:n0 + 8, 1:9]), ALU.add).then_inc(S(sem), 1)

            dve.wait_ge(S("evacuated"), Q[f"xnT{KD - 1}"] + 1)
            modulate(xnT, coefA, None, 0, 5, "h_ready")

            dve.wait_ge(S("evacuated"), Q["mqk1_3"] + 1)
            dve.wait_ge(S("xps_ready"), 1)
            for j in range(4):
                for k in range(KD):
                    wj = parT[:, k, j:j + 1]
                    outs = (qkT[:, k, 0:SEQ], qkT[:, k, SEQ:NTOK].rearrange("p (b t) -> p b t", b=NSEQ))
                    ins = (xpp[:, k, j:j + SEQ], xps[:, k, :, j:j + TS])
                    for y, x in zip(outs, ins):
                        if j == 0:
                            last = TSC(y, x, wj, parT[:, k, 4:5], ALU.mult, ALU.add)
                        else:
                            last = STT(y, x, wj, y, ALU.mult, ALU.add)
                if j < 3:
                    step(last)
                else:
                    last.then_inc(S("conv_done"), 1)

            ta = tmpA.rearrange("p h (u j) -> p h u j", u=2)
            tb = tmpB.rearrange("p h (u j) -> p h u j", u=2)
            for m, (name, z) in enumerate((("rq", rq), ("rk", rk))):
                for t in range(NT):
                    n = ROWS[t]
                    dve.wait_ge(S("evacuated"), Q[f"{name}_{t}"] + 1)
                    v = z[0:n, t, :].rearrange("p (h u j) -> p h u j", h=H, u=2)
                    cos = K("cos", NT, 64)[0:n, t, :]
                    sin = K("sin", NT, 64)[0:n, t, :].unsqueeze(1).to_broadcast([n, H, 64])
                    cosb = cos.unsqueeze(1).unsqueeze(1).to_broadcast([n, H, 2, 64])
                    TT(ta[0:n], v, cosb, ALU.mult)
                    TT(tb[0:n, :, 0, :], v[:, :, 1, :], sin, ALU.mult)
                    step(TT(tb[0:n, :, 1, :], v[:, :, 0, :], sin, ALU.mult))
                    TT(v[:, :, 0, :], ta[0:n, :, 0, :], tb[0:n, :, 0, :], ALU.subtract)
                    last = TT(v[:, :, 1, :], ta[0:n, :, 1, :], tb[0:n, :, 1, :], ALU.add)
                    if t < NT - 1:
                        step(last)
                last.then_inc(S("rotated"), 1)
                dve.wait_ge(S("rotated"), m + 1)

            dve.wait_ge(S("evacuated"), Q["gatesT"] + 1)
            dve.wait_ge(S("small_in"), 16 * SMALL)
            TT(gt["ipre"], gtok[:, :, 0:4], igf[:, 0:4].unsqueeze(1).to_broadcast([128, NT, H]), ALU.add)
            step(TT(gt["fpre"], gtok[:, :, 4:8], igf[:, 4:8].unsqueeze(1).to_broadcast([128, NT, H]), ALU.add))
            STT(gt["fabs"], gt["fpre"], -1.0, gt["fpre"], ALU.mult, ALU.max).then_inc(S("fabs_ready"), 1)
            dve.wait_ge(S("fexp"), 1)
            TSC(gt["fabs"], gt["fabs"], 1.0, None, ALU.add).then_inc(S("fabs_ready"), 1)
            dve.wait_ge(S("fexp"), 2)
            STT(gt["fpre"], gt["fpre"], 0.0, gt["fabs"], ALU.min, ALU.subtract).then_inc(S("logf_ready"), 1)

            dve.wait_ge(S("evacuated"), Q["rT7"] + 1)
            for t in range(NT):
                n = ROWS[t]
                v = rk[0:n, t, :].rearrange("p (h d) -> p h d", h=H)
                last = TT(v, v, K("kdec", NT, H)[0:n, t, :].unsqueeze(2).to_broadcast([n, H, HD]), ALU.mult)
            last.then_inc(S("keys_ready"), 1)

            b_, g_, M_ = gt["b"], gt["g"], gt["M"]
            dve.wait_ge(S("cumsum_done"), 1)
            dve.tensor_copy(b_[:, 0:2, :], psum[:, 0, 0:8].rearrange("p (t h) -> p t h", t=2))
            dve.tensor_copy(b_[0:64, 2, :], psum[0:64, 0, 8:12])
            step(dve.tensor_copy(gt["btot"][:, 0:2, :], psum[:, 0, 12:20].rearrange("p (t h) -> p t h", t=2)))
            step(TT(g_, gt["ipre"], b_, ALU.subtract))

            def diagonal(v, n):
                return TT(square_view(tmpA, n), ident[0:n, 0:n].unsqueeze(1).to_broadcast([n, H, n]),
                          v.unsqueeze(2).to_broadcast([n, H, n]), ALU.mult)

            for t in range(NT):
                n = ROWS[t]
                mask, maskT = (K("mask"), K("maskT")) if t < 2 else (K("maskS"), K("maskST"))
                diagonal(g_[0:n, t, :], n).then_inc(S("diag_ready"), 1)
                if t == 1:
                    TT(gt["mprev"][:, 1, :], gt["mlast"][:, 0, :], gt["btot"][:, 0, :], ALU.add)
                if t == 2:
                    dve.tensor_copy(gt["mprev"][0:64, 2, :], m0tok[0:64, :])
                dve.wait_ge(S("spread"), 2 * t + 1)
                if t:
                    dve.wait_ge(S("W_done"), t)
                tbv = square_view(tmpB, n)
                step(TT(tbv, psum[0:n, 1, 0:H * n].rearrange("p (h j) -> p h j", h=H),
                        mask[0:n, 0:n].unsqueeze(1).to_broadcast([n, H, n]), ALU.add))
                step(dve.reduce_max(M_[0:n, t, :], tbv, X))
                step(TT(M_[0:n, t, :], M_[0:n, t, :], gt["mprev"][0:n, t, :], ALU.max))
                TT(gt["mt"][0:n, t, :], b_[0:n, t, :], M_[0:n, t, :], ALU.add)
                diagonal(M_[0:n, t, :], n).then_inc(S("diag_ready"), 1)
                dve.wait_ge(S("spread"), 2 * t + 2)
                Mb = psum[:, 2, 0:H * n].rearrange("p (h j) -> p h j", h=H)
                if t < 2:
                    dve.tensor_copy(gt["mlast"][:, t, :].unsqueeze(2), Mb[:, :, n - 1:n])
                else:
                    dve.tensor_copy(mlS, Mb[:, :, TS - 1:n:TS])
                TT(tbv, maskT[0:n, 0:n].unsqueeze(1).to_broadcast([n, H, n]), Mb[0:n], ALU.subtract)\
                    .then_inc(S("W_in"), 1)
                dve.wait_ge(S("W_in"), t + 1)
            TT(gt["wint"], gt["mprev"], M_, ALU.subtract)
            TSC(gt["expm"], gt["mt"], -1.0, None, ALU.mult)
            TT(cdec[:, 0, 0:4], gt["mprev"][:, 1, :], gt["mlast"][:, 1, :], ALU.subtract)
            TT(cdec[:, 1, :].rearrange("p (b h) -> p b h", h=H), m0all, mlS.rearrange("p h b -> p b h"),
               ALU.subtract).then_inc(S("exps_in"), 1)
            dve.wait_ge(S("W_done"), NT)
            TSC(gt["wk"][:, 0:2, :].unsqueeze(3), Wm[:, 0:2, :, 127:128], SCALE, None, ALU.mult)
            step(dve.reduce_sum(gt["wk"][0:64, 2, :], Wm[0:64, 2, :, TS - 1:64:TS], X))
            step(TSC(gt["wk"][0:64, 2, :], gt["wk"][0:64, 2, :], SCALE, None, ALU.mult))
            for t in range(NT):
                n = ROWS[t]
                v = km[0:n, t, :].rearrange("p (h d) -> p h d", h=H)
                last = TT(v, v, gt["wk"][0:n, t, :].unsqueeze(2).to_broadcast([n, H, HD]), ALU.mult)
            last.then_inc(S("keys_ready"), 1)
            dve.wait_ge(S("exps_done"), 1)

            def pair_view(bank0, n, w):
                return psum[0:n, bank0:bank0 + 2, 0:258].rearrange("p b (h e) -> p b h e", h=2)[:, :, :, 0:w]

            for g, (kind, t) in enumerate(GROUPS):
                n = ROWS[t]
                w = HD + kind
                dve.wait_ge(S("scored"), g + 1)
                if g:
                    dve.wait_ge(S("intra_done"), g)
                bank = 0 if g % 2 == 0 else 7
                sc = psum[0:n, bank, 0:H * n].rearrange("p (h i) -> p h i", h=H)
                if kind:
                    STT(sT[0:n, :, 0:n], sc, SCALE, Wm[0:n, t, :, 0:n], ALU.mult, ALU.mult).then_inc(S("sT_ready"), 1)
                else:
                    dec = K("decT", H, 128) if t < 2 else K("decTS", H, 64)
                    TT(sT[0:n, :, 0:n], sc, dec[0:n], ALU.mult).then_inc(S("sT_ready"), 1)

                def carry_prompt():
                    dve.wait_ge(S("state_done"), g + 1)
                    cs = Cst[:, kind].rearrange("p (a h) e -> p a h e", a=2)[:, :, :, 0:w]
                    if t == 0:
                        dve.tensor_copy(cs, pair_view(5, 128, w)).then_inc(S("carried"), 1)
                        return
                    dve.wait_ge(S("inter_done"), kind + 1)
                    for h in range(H):
                        dec = float(np.exp(lg[h] * np.float32(128))) if kind == 0 else cdec[:, 0, h:h + 1]
                        last = STT(Cst[:, kind, h, 0:w], Cst[:, kind, h, 0:w], dec,
                                   psum[:, 5 + h // 2, 129 * (h % 2):129 * (h % 2) + w], ALU.mult, ALU.add)
                    last.then_inc(S("carried"), 1)

                def carry_samples():
                    for h in range(H):
                        i = kind * H + h
                        dve.wait_ge(S("stateS_done"), i + 1)
                        ps = psum[:, 5:7, :].rearrange("p a (b e) -> p (a b) e", e=HD)
                        s0 = S0[:, i % 2, :, 0:HD]
                        if kind == 0:
                            dec = float(np.exp(lg[h] * np.float32(TS)))
                            last = STT(s0, s0, dec, ps, ALU.mult, ALU.add)
                        else:
                            for b in range(NSEQ):
                                STT(s0[:, b, :], s0[:, b, :], cdec[:, 1, H * b + h:H * b + h + 1], ps[:, b, :],
                                    ALU.mult, ALU.add)

                            def nh(k):
                                return nT[:, k, :].rearrange("p (b h) -> p b h", h=H)[:, :, h]
                            step(TT(nh(1), nh(0), cdec[:, 1, :].rearrange("p (b h) -> p b h", h=H)[:, :, h], ALU.mult))
                            last = TT(nh(1), nh(1), psum[:, 0, NSEQ * h:NSEQ * h + NSEQ], ALU.add)
                        last.then_inc(S("carriedS"), 1)

                carry_prompt() if t < 2 else carry_samples()
                dve.wait_ge(S("intra_done"), g + 1)
                cv = comb[0:n].rearrange("p (a h) e -> p a h e", a=2)[:, :, :, 0:w]
                if t == 0:
                    dve.tensor_copy(cv, pair_view(1, n, w)).then_inc(S("combined"), 1)
                else:
                    dve.wait_ge(S("inter_done"), (kind + 1) if t == 1 else 2 + H * (kind + 1))
                    dec = gt["wint"][0:n, t, :] if kind else K("qdec", NT, H)[0:n, t, :]
                    step(TT(cv, pair_view(3, n, w), dec.rearrange("p (a h) -> p a h", a=2).unsqueeze(3)
                            .to_broadcast([n, 2, 2, w]), ALU.mult))
                    TT(cv, cv, pair_view(1, n, w), ALU.add).then_inc(S("combined"), 1)
                dve.wait_ge(S("combined"), g + 1)
                y = comb[0:n, :, 0:HD]
                if kind:
                    den = comb[0:n, :, HD]
                    d = stat[0:n, 4:8]
                    step(STT(d, den, -1.0, den, ALU.mult, ALU.max))
                    step(TT(d, d, gt["expm"][0:n, t, :], ALU.max))
                    step(dve.reciprocal(d, d))
                    step(TT(y, y, d.unsqueeze(2).to_broadcast([n, H, HD]), ALU.mult))
                for h in range(H):
                    last = dve.bn_stats(stat[0:n, 16 + 6 * h:22 + 6 * h], comb[0:n, h, 0:HD])
                step(last)
                if g:
                    dve.wait_ge(S("head_rstd"), g)
                for h in range(H):
                    last = dve.bn_aggr(mv2[0:n, h, :], stat[0:n, 16 + 6 * h:22 + 6 * h])
                last.then_inc(S("moments"), 1)
                dve.wait_ge(S("head_rstd"), g + 1)
                for h in range(H):
                    last = TSC(nrm[0:n, h, :], comb[0:n, h, 0:HD], mv2[0:n, h, 0:1], hr[0:n, h:h + 1],
                               ALU.subtract, ALU.mult)
                step(last)
                if g == 0:
                    dve.wait_ge(S("gates_scaled"), 1)
                z = (mo if kind else rg)[0:n, t, :].rearrange("p (h d) -> p h d", h=H)
                TT(z, nrm[0:n], z, ALU.mult).then_inc(S("y_ready"), 1)

            dve.wait_ge(S("x2_in"), 32)
            dve.wait_ge(S("evac2"), KD + 6)
            for t in range(NT):
                n = ROWS[t]
                for u in range(2):
                    i = 2 * t + u
                    dve.wait_ge(S("outproj"), i + 1)
                    xs = x2[0:n, t, 512 * u:512 * u + 512]
                    ga = gateA[0:n, t, 512 * u:512 * u + 512]
                    step(TT(ga, psum[0:n, 6 + u, :], ga, ALU.mult))
                    TT(xs, xs, ga, ALU.add).then_inc(S("residual"), 1)
            dve.wait_ge(S("rstd_ready"), 2)
            for t in range(NT):
                TSC(yfin[0:ROWS[t], t, :], x2[0:ROWS[t], t, :], rs[0:ROWS[t], t:t + 1], None, ALU.mult)\
                    .then_inc(S("xn2_ready"), 1)
            dve.wait_ge(S("evac2"), 2 * KD + 12)
            modulate(xnT2, coefF, None, 24, 6, "h2_ready")
            for t in range(NT):
                n = ROWS[t]
                b = 2 * (t % 2)
                dve.wait_ge(S("part"), 3 * t + 1)
                r = yfin[0:n, t, :]
                TT(r, psum[0:n, b:b + 2, :].rearrange("p b n -> p (b n)"), h2p[0:n, 0, t, :], ALU.subtract)\
                    .then_inc(S("rest"), 1)
                dve.wait_ge(S("part"), 3 * t + 2)
                TT(r, r, h2p[0:n, 1, t, :], ALU.subtract).then_inc(S("rest"), 1)
            dve.wait_ge(S("logits"), 1)
            for t in range(NT):
                n = ROWS[t]
                TT(logit[0:n, t, :], psum[0:n, 7, 32 * t:32 * t + 32], brout[0:n, :], ALU.add)\
                    .then_inc(S("dve_r"), 1)
            dve.wait_ge(S("dve_r"), NT)
            for t in range(NT):
                last = dve.max(top8[0:ROWS[t], t, :], logit[0:ROWS[t], t, :])
            step(last)
            for t in range(NT):
                dve.max_index(idx8[0:ROWS[t], t, :], top8[0:ROWS[t], t, :], logit[0:ROWS[t], t, :])
                last = TSC(nmax[0:ROWS[t], t:t + 1], top8[0:ROWS[t], t, 0:1], -1.0, None, ALU.mult)
            last.then_inc(S("softmax_in"), 1)
            dve.wait_ge(S("softmax_in"), 1)
            for t in range(NT):
                last = dve.tensor_copy(idxf[0:ROWS[t], t, :], idx8[0:ROWS[t], t, :])
            step(last)
            for k in range(4):
                for t in range(NT):
                    n = ROWS[t]
                    if k == 0:
                        last = TSC(route[0:n, t, :], K("eidx")[0:n, :], idxf[0:n, t, 0:1], None, ALU.is_equal)
                    else:
                        last = STT(route[0:n, t, :], K("eidx")[0:n, :], idxf[0:n, t, k:k + 1], route[0:n, t, :],
                                   ALU.is_equal, ALU.add)
                if k < 3:
                    step(last)
            last.then_inc(S("route_ready"), 1)
            dve.wait_ge(S("route_ready"), 1)
            dve.wait_ge(S("softmax_exp"), 1)
            for t in range(NT):
                n = ROWS[t]
                step(TT(pexp[0:n, t, :], pexp[0:n, t, :], route[0:n, t, :], ALU.mult))
                step(dve.reduce_sum(nmax[0:n, t:t + 1], pexp[0:n, t, :], X))
                step(dve.reciprocal(nmax[0:n, t:t + 1], nmax[0:n, t:t + 1]))
                step(TSC(gate[0:n, t, 0:NE], pexp[0:n, t, :], nmax[0:n, t:t + 1], None, ALU.mult))
            dve.wait_ge(S("places"), 1)
            step(dve.memset(pos, 0.0))
            for t in range(NT):
                n = ROWS[t]
                last = TT(pos[0:n, t, 0:NE], psum[0:n, 6, 32 * t:32 * t + 32], route[0:n, t, :], ALU.mult)
            step(last)
            step(TSC(pos, pos, -1.0, None, ALU.add))
            step(dve.tensor_copy(counts[:, 0:NE], psum[:, 6, 96:128]))
            step(dve.reduce_max(counts[:, NE:NE + 1], counts[:, 0:NE], X))
            dve.tensor_copy(counts_i, counts).then_inc(S("counts_ready"), 1)
            dve.wait_ge(S("part"), 3 * NT)
            dve.memset(acc, 0.0).then_inc(S("added"), 1)
            dve.wait_ge(S("added"), 1)
            dve.wait_ge(S("P_zero"), 1)

            def one_hot(r, e, i):
                if not isinstance(i, int) or i > 0:
                    dve.wait_ge(S("gathered"), i)
                sl = K("slots")[:, bass.ds(r * 128, 128)] if not isinstance(r, int) else \
                    K("slots")[:, r * 128:r * 128 + 128]
                for t in range(NT):
                    n = ROWS[t]
                    last = TSC(P[0:n, t, :], sl[0:n, :], pos[0:n, t, bass.ds(e, 1)], None, ALU.is_equal)
                last.then_inc(S("P_ready"), 1)

            def expert(r, e, it, count):
                ig = r * (NE + 1) + e
                one_hot(r, e + 1, ig + 1)

                def weighted(slots):
                    first = r * 128 if isinstance(r, int) else None
                    sl = K("slots")[:, bass.ds(r * 128, 128)] if first is None else K("slots")[:, first:first + slots]
                    for t in range(NT):
                        n = ROWS[t]
                        last = TSC(Pg[0:n, t, :].rearrange("p (q s) -> p q s", s=slots),
                                   sl[0:n, :].unsqueeze(1).to_broadcast([n, 128 // slots, slots]),
                                   pos[0:n, t, bass.ds(e, 1)], gate[0:n, t, bass.ds(e, 1)], ALU.is_equal, ALU.mult)
                    last.then_inc(S("Pg_ready"), 1)

                def swiglu(slots):
                    n = 8 * slots
                    g_, s_, l_ = (v.rearrange("p u n -> p (u n)")[:, 0:n] for v in (gt_, sg, li))
                    gate_in = flat(0, n)
                    lin_in = psum[:, 0, 256:512] if slots == 32 else flat(slots // 64, n)
                    dve.wait_ge(S("up_done"), it + 1)
                    TSC(g_, gate_in, 7.0, None, ALU.min).then_inc(S("gate_ready"), 1)
                    TSC(l_, lin_in, 7.0, -7.0, ALU.min, ALU.max).then_inc(S("lin_clipped"), 1)
                    dve.wait_ge(S("lin_clipped"), it + 1)
                    dve.wait_ge(S("gate_ready"), it + 1)
                    STT(l_, l_, 1.0, g_, ALU.add, ALU.mult).then_inc(S("lin_gated"), 1)
                    dve.wait_ge(S("lin_gated"), it + 1)
                    dve.wait_ge(S("sig_ready"), it + 1)
                    TT(g_, l_, s_, ALU.mult).then_inc(S("act_ready"), 1)

                by_size(dve, count, weighted)
                by_size(dve, count, swiglu)
                add_scattered(it)

            def add_scattered(it):
                for t in range(NT):
                    dve.wait_ge(S("scattered"), 3 * it + t + 1)
                    v = acc[:, t, :] if t < 2 else acc[:, 2, 0:512]
                    src = flat((6, 4, 6)[t], D if t < 2 else 512)
                    TT(v, v, src, ALU.add).then_inc(S("added"), 1)
                dve.wait_ge(S("added"), 3 * it + 4)

            one_hot(0, 0, 0)
            with dve.Fori(0, NE) as e:
                count = dve.value_load(counts_i[0:1, bass.ds(e, 1)], min_val=0, max_val=NTOK)
                expert(0, e, e, count)
            most = dve.value_load(counts_i[0:1, NE:NE + 1], min_val=0, max_val=NTOK)
            with dve.If(most > BIG_BLOCK):
                with dve.Fori(1, ROUNDS) as r:
                    one_hot(r, 0, r * (NE + 1))
                    with dve.Fori(0, NE) as e:
                        expert(r, e, r * NE + e, None)
                add_scattered(NE * ROUNDS)
            with dve.Else():
                add_scattered(NE)
            dve.tensor_copy(acc[0:64, 2, 512:D], acc[64:128, 2, 0:512]).then_inc(S("moe_done"), 1)
            dve.wait_ge(S("moe_done"), 1)
            for t in range(NT):
                n = ROWS[t]
                step(TT(acc[0:n, t, :], acc[0:n, t, :], gateF[0:n, t, :], ALU.mult))
                TT(x2[0:n, t, :], x2[0:n, t, :], acc[0:n, t, :], ALU.add).then_inc(S("x3_ready"), 1)
            dve.wait_ge(S("gfin_in"), 16)
            for t in range(NT):
                n = ROWS[t]
                dve.wait_ge(S("rstd3"), t + 1)
                STT(x2[0:n, t, :], x2[0:n, t, :], rs[0:n, t:t + 1], gfin.rearrange("p u n -> p (u n)")[0:n, :],
                    ALU.mult, ALU.mult).then_inc(S("y_final"), 1)


_OUTS = [("y_prompt", (1, SEQ, D)), ("y_sample", (NSEQ, TS, D)),
         ("ret_p", (1, 1, H, HD, HD)), ("c_p", (1, 1, H, HD, HD)), ("n_p", (1, 1, H, HD)), ("m_p", (1, 1, H)),
         ("conv_p", (1, 1, 3, D)),
         ("ret_s", (1, NSEQ, H, HD, HD)), ("c_s", (1, NSEQ, H, HD, HD)), ("n_s", (1, NSEQ, H, HD)),
         ("m_s", (1, NSEQ, H)), ("conv_s", (1, NSEQ, 3, D))]


def kernel(**inputs):
    import concourse.bacc as bacc
    from concourse.bass_utils import run_bass_kernel_spmd

    nc = bacc.Bacc("TRN2", target_bir_lowering=False, num_devices=1)
    arrays, aps = {}, {}

    def give(name, v):
        v = np.ascontiguousarray(v)
        arrays[f"in_{name}"] = v
        aps[name] = nc.dram_tensor(f"in_{name}", v.shape, mybir.dt.from_np(v.dtype), kind="ExternalInput").ap()

    for name, v in inputs.items():
        give(name, v)
    give("tables", np.concatenate(list(constant_tables().values()), axis=1))
    give("selectors", gate_selectors())
    for name, shape in _OUTS:
        aps[name] = nc.dram_tensor(f"out_{name}", shape, mybir.dt.float32, kind="ExternalOutput").ap()
    build(nc, aps)
    r = run_bass_kernel_spmd(nc, [arrays], core_ids=[0])
    return tuple(r.results[0][f"out_{name}"] for name, _ in _OUTS)
```

```python
import numpy as np
import concourse.bass as bass
from concourse import mybir
from contextlib import ExitStack

D = 1024
KD = D // 128
SEQ, NSEQ, TS = 256, 8, 8
NTOK = SEQ + NSEQ * TS
NT = 3
ROWS = [128, 128, 64]
H = 4
HD = 128
NE = 32
EPS = 1e-6
SCALE = HD ** -0.5
NEG = -1e30
PAST = 2048
BIG_BLOCK = 128
SIZES = (32, 64, 128)
ROUNDS = -(-NTOK // BIG_BLOCK)
SLOT = 4096


def log_gamma():
    return np.log1p(-np.exp2(-5.0 - np.arange(H, dtype=np.float32))).astype(np.float32)


def constant_tables():
    f = np.float32
    i = np.arange(128)
    t = {}
    t["ident"] = np.eye(128, dtype=f)
    t["ones"] = np.ones((128, 128), f)
    low = i[None, :] <= i[:, None]
    same = (i[:, None] // TS) == (i[None, :] // TS)
    t["mask"] = np.where(low, 0, NEG).astype(f)
    t["maskT"] = np.ascontiguousarray(t["mask"].T)
    t["tri"] = low.T.astype(f)
    sm = np.where(low & same, 0, NEG).astype(f)
    t["maskS"] = sm[:, :64].copy()
    t["maskST"] = np.ascontiguousarray(sm.T)[:, :64].copy()
    t["triS"] = (low & same).T.astype(f)[:, :64].copy()
    lg = log_gamma()
    rel = (i[None, :] - i[:, None]).astype(f)
    dec = np.exp(lg[:, None, None] * np.maximum(rel, 0)) * (rel >= 0)
    t["decT"] = (dec * f(SCALE)).astype(f).transpose(1, 0, 2).reshape(128, H * 128)
    t["decTS"] = (dec * f(SCALE) * same).astype(f).transpose(1, 0, 2)[:, :, :64].reshape(128, H * 64)
    pos = np.stack([i, i + 128, PAST + i % TS], 1).astype(f)
    inv = np.power(f(10000.0), -np.arange(64, dtype=f) / f(64)).astype(f)
    ang = (pos[:, :, None] * inv).astype(f)
    t["cos"] = np.cos(ang).astype(f).reshape(128, NT * 64)
    t["sin"] = np.sin(ang).astype(f).reshape(128, NT * 64)
    idx = np.stack([i, i, i % TS], 1).astype(f)
    length = np.array([128, 128, TS], f)
    t["qdec"] = np.exp(lg * (idx[:, :, None] + 1)).astype(f).reshape(128, NT * H)
    t["kdec"] = (np.exp(lg * (length[None, :, None] - 1 - idx[:, :, None])) * f(SCALE)).astype(f).reshape(128, NT * H)
    t["seqmask"] = ((i[:, None] // TS) == np.arange(NSEQ)[None, :]).astype(f)
    t["slots"] = np.tile(np.arange(ROUNDS * 128, dtype=f), (128, 1))
    t["biasrow"] = ((i[:, None] % 32 == np.arange(33)[None, :] % NE) & (i[:, None] // 32 != 1)).astype(f)
    t["eidx"] = np.tile(np.arange(32, dtype=f), (128, 1))
    return {k: np.ascontiguousarray(v.astype(f)) for k, v in t.items()}


def gate_selectors():
    s = np.zeros((128, 4, NTOK), np.float32)
    cond = np.concatenate([np.zeros(SEQ, int), 1 + np.arange(NSEQ * TS) // TS])
    for t in range(4):
        s[32 * t + cond, t, np.arange(NTOK)] = 1
    return s.reshape(128, 4 * NTOK)


def build(nc, a):
    F32, BF, I32, U32 = mybir.dt.float32, mybir.dt.bfloat16, mybir.dt.int32, mybir.dt.uint32
    ALU, ACT, AX = mybir.AluOpType, mybir.ActivationFunctionType, mybir.AxisListType
    X = AX.X
    tabs = constant_tables()
    lg = log_gamma()
    ctx = ExitStack()
    with ctx:
        WORDS = 53100
        mem = ctx.enter_context(nc.sbuf_tensor("mem", [128, WORDS], F32))
        psum = ctx.enter_context(nc.psum_tensor("psum", [128, 8, 512], F32))

        def at(off, *shape):
            n = int(np.prod(shape))
            assert off + n <= WORDS, (off, shape)
            v = mem[:, off:off + n]
            if len(shape) == 1:
                return v
            names = "abcd"[:len(shape)]
            return v.rearrange(f"p ({' '.join(names)}) -> p {' '.join(names)}",
                               **{k: s for k, s in zip(names, shape)})

        def at_bf(off, *shape):
            n = int(np.prod(shape))
            v = mem[:, off:off + n // 2].bitcast(BF)
            if len(shape) == 1:
                return v
            names = "abcd"[:len(shape)]
            return v.rearrange(f"p ({' '.join(names)}) -> p {' '.join(names)}",
                               **{k: s for k, s in zip(names, shape)})

        def slot8(s):
            return at(s * SLOT, 8, 512)

        cursor = [6 * SLOT]

        def take(n):
            o = cursor[0]
            cursor[0] += n
            assert cursor[0] <= WORDS, cursor[0]
            return o

        const_off = {}
        C0 = cursor[0]
        for k, v in tabs.items():
            const_off[k] = take(v.shape[1])
        CW = cursor[0] - C0

        def K(name, *shape):
            v = tabs[name]
            return at(const_off[name], *(shape or (v.shape[1],)))

        ident = K("ident")
        ones = K("ones")
        cT = at(take(KD * 32), KD, 32)
        parT = at(take(KD * 32), KD, 32)
        coefA = at(take(KD * 9), KD, 9)
        coefF = at(take(KD * 9), KD, 9)
        stat = at(take(160), 160)
        gt = {k: at(take(NT * H), NT, H) for k in
              ("ipre", "fpre", "fabs", "b", "g", "M", "mt", "mprev", "wint", "expm", "wk", "btot", "mlast")}
        igf = at(take(16), 16)
        m0all = at(take(32), NSEQ, H)
        m0tok = at(take(4), 4)
        cdec = at(take(64), 2, 32)
        nT = at(take(64), 2, 32)
        wg = at(take(KD * 8), KD, 8)
        wr = at(take(KD * NE), KD, NE)
        pos = at(take(NT * 33), NT, 33)
        gate = at(take(NT * 33), NT, 33)
        route = at(take(NT * NE), NT, NE)
        brout = at(take(NE), NE)
        counts = at(take(33), 33)
        counts_i = mem[:, cursor[0]:cursor[0] + 33].bitcast(I32)
        take(33)
        hr = at(take(4), 4)
        mv2 = at(take(8), H, 2)
        top8 = at(take(24), NT, 8)
        idx8 = mem[:, cursor[0]:cursor[0] + 24].bitcast(U32).rearrange("p (t k) -> p t k", t=NT)
        take(24)
        idxf = at(take(24), NT, 8)
        nmax = at(take(4), 4)
        logit = at(take(96), NT, 32)
        pexp = at(take(96), NT, 32)
        ss = at(take(8), 8)
        halves = at(take(4), 4)
        rs = at(take(8), 8)
        B0 = cursor[0]

        o = B0
        hT = at(o, KD, NTOK)
        comb = at(o + 1024, H, HD + 1)
        nrm = at(o + 1540, H, 128)
        xg = at(o, KD, 128)
        Pg = at(o + 1024, NT, 128); G = at(o + 1408, NTOK); P = at_bf(o + 1728, NT, 128)
        bsel = at_bf(o + 1920, 128)
        o += KD * NTOK
        modr = at(o, 12, 128)
        bparts = at_bf(o, 3 * D)
        o += 1536
        modT = at(o, 48, 9); o += 432
        rk = at(o, NT, 512); rv = at(o + 1536, NT, 512); yfin = at(o, NT, D); prow = at(o + 1536, D)
        acc = yfin; gateA = yfin; o += 3072
        mo = at(o, NT, 512); rg = at(o + 1536, NT, 512); xin = at(o, NT, D)
        h2p = at_bf(o, 3, NT, D); o += 3072
        rq = at(o, NT, 512); crow = at(o, D); o += 1536
        gateF = at(o, NT, D)
        gnorm = at(o, 2, 512)
        xpp = at(o, KD, 3 + SEQ); xps = at(o + KD * (3 + SEQ), KD, NSEQ, 3 + TS)
        o += KD * (3 + SEQ) + KD * NSEQ * (3 + TS)
        o5 = o
        qkT = at(o, KD, NTOK); o += KD * NTOK
        rT = at(o, KD, NTOK); xnT = rT; o += KD * NTOK
        x2 = at(o5 + 296, NT, D)
        sel = at(o5 + 3368, 4, NTOK)
        xnT2 = at(o5 + 4648, KD, NTOK); lgT = at(o5 + 4648, NTOK)
        gt_ = at(o5 + 3368, 2, 512); sg = at(o5 + 4392, 2, 512); li = at(o5 + 5416, 2, 512)
        actT = at(o5 + 6440, KD, 128); yd = at(o5 + 7464, 2, 512)
        gfin = li
        assert o5 + 7464 + 1024 <= WORDS, o5 + 8488
        vaug = at(o, NT, H, HD + 1); o += NT * H * (HD + 1)
        Wm = at(o, NT, H, 128); o += 1536
        tmpA = at(o, H, 128); o += 512
        assert o <= WORDS, o
        o = 4 * SLOT
        S0_near = at(o, 2, NSEQ, HD + 1); bmod = at(o, 12, 128); o += 2 * NSEQ * (HD + 1)
        QM = at(o, 2, NSEQ, 72); QMF = at(o, 2, 576); o += 1152
        vmask0 = at(o, NSEQ, HD); convrow = at(o, D); lgTm = at(o, NTOK); o += 1024
        Cst = at(o, 2, H, HD + 1); o += 2 * H * (HD + 1)
        sT = at(o, H, 128); cbuf = at(o, KD, 27); o += 512
        tmpB = at(o, H, 128); o += 512
        km = at(o, NT, 512); o += 1536
        gtok = at(o, NT, 8); o += 24
        nrow = at(o, 128); o += 128
        mlS = at(o, H, NSEQ); o += 32
        assert o <= 6 * SLOT, o

        brows = at(4 * SLOT, 3 * D)

        def vmask(i):
            return vmask0 if i % 2 == 0 else at(2 * SLOT + 6 * NSEQ * (HD + 1), NSEQ, HD)

        def S0(i):
            return S0_near[:, i] if i < 2 else at(2 * SLOT + (i - 2) * NSEQ * (HD + 1), NSEQ, HD + 1)

        SMALL, STORES = 14, 6
        EARLY = 3
        SPLIT = [(0, 0), (1, 0), (0, 1), (2, 0), (1, 1), (0, 2), (2, 1), (1, 2), (2, 2)]

        def square_view(v, n):
            return v.rearrange("p h j -> p (h j)")[0:n, 0:H * n].rearrange("p (h j) -> p h j", h=H)

        def tmpA_v(n):
            return tmpA.rearrange("p h j -> p (h j)")[0:n, 0:H * n]

        sems = {}

        def S(name):
            if name not in sems:
                sems[name] = ctx.enter_context(nc.semaphore(name))
            return sems[name]

        loaded = [S(f"slot{c}_loaded") for c in range(6)]
        used = [S(f"slot{c}_used") for c in range(6)]

        def by_size(eng, count, f):
            if count is None:
                f(SIZES[2])
                return
            with eng.If(count <= SIZES[0]):
                f(SIZES[0])
            with eng.Else():
                with eng.If(count <= SIZES[1]):
                    f(SIZES[1])
                with eng.Else():
                    f(SIZES[2])

        def flat(bank0, n):
            return psum[:, bank0:bank0 + -(-n // 512), :].rearrange("p b n -> p (b n)")[:, 0:n]

        def chained(eng, name):
            n = [0]

            def step(ins):
                n[0] += 1
                ins.then_inc(S(name), 1)
                eng.wait_ge(S(name), n[0])
            return step

        COL = {"rq": 0, "rk": 512, "rv": 1024, "rg": 1536, "mqk0": 2048, "mqk1": 2560, "mv": 3072, "mo": 3584}
        CH = (["mod0", "mod1", "mod2", "mod3", "mqk0", "mod4", "mqk1", "mod5", "rq", "mod6", "rk", "mod7",
               "mv", "mod8", "rv", "mod9", "mo", "mod10", "rg", "mod11", "out0", "out1"])
        NCH = len(CH)
        USES = [len(range(c, NCH, 4)) if c < 4 else 0 for c in range(6)]

        def chunk_source(name):
            if name.startswith("mod"):
                w, c = a["w_mod"][0], 512 * int(name[3:])
            elif name.startswith("out"):
                w, c = a["w_out"][0], 512 * int(name[3:])
            else:
                w, c = a["w_in"][0], COL[name]
            return w[:, c:c + 512].rearrange("(k p) n -> p k n", p=128)

        BANKS = 6
        OUTS = ["c"] + [f"mod{n}" for n in range(4)] + [f"modT{n}" for n in range(4)] + ["par", "nstate"]
        OUTS += [f"xnT{k}" for k in range(KD)]
        for n in range(4, 20):
            c = CH[n]
            if c.startswith("mod"):
                OUTS.append(c)
            elif c.startswith("mqk"):
                OUTS += [f"{c}_{m}" for m in range(4)]
                if c == "mqk1":
                    OUTS += ["gates", "gatesT"]
            else:
                OUTS += [f"{c}_{t}" for t in range(NT)]
                if c == "mv":
                    OUTS += [f"km{t}" for t in range(NT)] + ["conv0", "conv1"]
                if c == "rv":
                    OUTS += [f"rT{h}" for h in range(2 * H)]
        OUTS += [f"modT{n}" for n in (6, 7, 8, 9)]
        Q = {n: q for q, n in enumerate(OUTS)}
        NQ = len(OUTS)
        GROUPS = [(0, 0), (1, 0), (0, 1), (1, 1), (0, 2), (1, 2)]

        def tok(t):
            return slice(128 * t, 128 * t + ROWS[t])

        block = ctx.enter_context(nc.Block())

        @block.sync
        def _(sp):
            sp.dma_start(crow[0:1, :], a["c_prompt"]).then_inc(S("c_in"), 16)
            sp.dma_start(crow[1:9, :], a["c_sample"]).then_inc(S("c_in"), 16)
            sp.dma_start(ident, a["tables"][:, 0:128]).then_inc(S("tables_in"), 16)
            for n in range(3):
                sp.dma_start(slot8(n), chunk_source(CH[n])).then_inc(loaded[n], 16)
            sp.dma_start(xin[:, 0:2, :], a["x_prompt"][0].rearrange("(t p) d -> p t d", p=128)).then_inc(S("x_in"), 16)
            sp.dma_start(xin[0:64, 2, :], a["x_sample"].rearrange("b t d -> (b t) d")).then_inc(S("x_in"), 16)
            for n in range(3, NCH):
                if n == 6:
                    sp.dma_start(at(C0 + 128, CW - 128), a["tables"][:, 128:CW]).then_inc(S("more_tables_in"), 16)
                if n >= 4:
                    sp.wait_ge(used[n % 4], n // 4)
                sp.dma_start(slot8(n % 4), chunk_source(CH[n])).then_inc(loaded[n % 4], 16)

            def load_state(i):
                src = a["state_mlstm_c"] if i >= H else a["state_ret"]
                sp.dma_start(S0(i)[:, :, 0:HD], src[0][:, i % H].rearrange("b d e -> d b e"))\
                    .then_inc(S(f"S0_in{i}"), 16)

            for c in (2, 3):
                sp.wait_ge(used[c], USES[c])
            for i in range(2, 2 * H):
                load_state(i)
            sp.wait_ge(S("mod_biased"), 12)
            load_state(0)
            load_state(1)

            def expert_chunk(e, c):
                if c < 4:
                    src = a["w_up"][0][e, 256 * c:256 * (c + 1), :].rearrange("(j p) n -> p j n", p=128)
                    dst = at(c * SLOT, 2, 2 * D)
                else:
                    src = a["w_down"][0][e, 512 * (c - 4):512 * (c - 3), :].rearrange("(j p) n -> p j n", p=128)
                    dst = at(c * SLOT, 4, D)
                sp.dma_start(dst, src).then_inc(loaded[c], 16)

            sp.wait_ge(S("S0_out"), 16 * 2 * H)
            for c in (2, 3, 5, 0, 1, 4):
                if c < 4:
                    sp.wait_ge(used[c], USES[c])
                elif c == 5:
                    sp.wait_ge(S("y_ready"), len(GROUPS))
                    sp.wait_ge(S("state_out"), 16 * STORES)
                else:
                    sp.wait_ge(S("bias_split"), 1)
                expert_chunk(0, c)
            with sp.Fori(1, NE) as e:
                for c in range(6):
                    sp.wait_ge(used[c], e + USES[c])
                    expert_chunk(e, c)
            sp.wait_ge(S("counts_ready"), 1)
            most = sp.value_load(counts_i[0:1, NE:NE + 1], min_val=0, max_val=NTOK)
            with sp.If(most > BIG_BLOCK):
                with sp.Fori(1, ROUNDS) as r:
                    with sp.Fori(0, NE) as e:
                        for c in range(6):
                            sp.wait_ge(used[c], r * NE + e + USES[c])
                            expert_chunk(e, c)
            with sp.Else():
                sp.nop()
            sp.wait_ge(S("y_out"), 16 * 2)
            sp.wait_ge(S("state_out"), 16 * STORES)

        @block.tensor
        def _(pe):
            def bank_free(q):
                if q >= BANKS:
                    pe.wait_ge(S("evacuated"), q - BANKS + 1)

            def take_chunk(n):
                pe.wait_ge(loaded[n % 4], 16 * (n // 4 + 1))
                return slot8(n % 4)

            pe.wait_ge(S("tables_in"), 16)
            pe.wait_ge(S("c_silu"), 1)
            for k in range(KD):
                last = pe.transpose(psum[:, 0, 32 * k:32 * k + 9], crow[0:9, 128 * k:128 * k + 128], ident[0:9, 0:9])
            last.then_inc(S("projected"), 1)

            def mod_rows(name, n):
                q = Q[name]
                w = take_chunk(n)
                bank_free(q)
                for k in range(KD):
                    for t in range(4):
                        last = pe.matmul(psum[32 * t:32 * t + 32, q % BANKS, 0:128], cT[:, k, :],
                                         w[:, k, 128 * t:128 * t + 128], start=(k == 0), stop=(k == KD - 1))
                last.then_inc(used[n % 4], 1)
                pe.wait_ge(used[n % 4], n // 4 + 1)
                pe.nop().then_inc(S("projected"), 1)

            def mod_transposed(n):
                q = Q[f"modT{n}"]
                bank_free(q)
                pe.wait_ge(S("mod_biased"), n + 1)
                pe.transpose(psum[:, q % BANKS, 0:128], modr[:, n, :], ident).then_inc(S("projected"), 1)

            def cumulate():
                pe.wait_ge(S("logf_ready"), 1)
                for t in range(NT):
                    n = ROWS[t]
                    tri = K("tri") if t < 2 else K("triS")
                    pe.matmul(psum[0:n, 6, 4 * t:4 * t + 4], tri[0:n, 0:n], gt["fpre"][0:n, t, :], start=True, stop=True)
                for t in range(2):
                    last = pe.matmul(psum[:, 6, 12 + 4 * t:16 + 4 * t], ones, gt["fpre"][:, t, :], start=True, stop=True)
                last.then_inc(S("cumsum_done"), 1)

            def spread(t, row):
                n = ROWS[t]
                pe.wait_ge(S("diag_ready"), 2 * t + row + 1)
                pe.matmul(psum[0:128 if row else n, 6 + row, 0:H * n], ones[0:n, 0:128 if row else n], tmpA_v(n),
                          start=True, stop=True).then_inc(S("spread"), 1)

            SPREADS = {("rv", 0): (0, 0), ("rv", 1): (0, 1), ("mo", 0): (1, 0), ("mo", 1): (1, 1),
                       ("rg", 0): (2, 0), ("rg", 1): (2, 1)}
            pe.wait_ge(S("evacuated"), 1)
            for n in range(4):
                mod_rows(f"mod{n}", n)
            for n in range(4):
                mod_transposed(n)
            pe.wait_ge(S("params_in"), 16 * 5)
            q = Q["par"]
            bank_free(q)
            for k in range(KD):
                last = pe.transpose(psum[:, q % BANKS, 31 * k:31 * k + 31], prow[0:31, 128 * k:128 * k + 128],
                                    ident[0:31, 0:31])
            last.then_inc(S("projected"), 1)
            pe.wait_ge(S("nstate_in"), 16)
            q = Q["nstate"]
            bank_free(q)
            pe.transpose(psum[:, q % BANKS, 0:32], nrow[0:32, :], ident[0:32, 0:32]).then_inc(S("projected"), 1)
            pe.wait_ge(S("xn_ready"), 3)
            for k in range(KD):
                q = Q[f"xnT{k}"]
                bank_free(q)
                for t in range(NT):
                    last = pe.transpose(psum[:, q % BANKS, tok(t)], xin[0:ROWS[t], t, 128 * k:128 * k + 128],
                                        ident[0:ROWS[t], 0:ROWS[t]])
                last.then_inc(S("projected"), 1)
            pe.wait_ge(S("h_ready"), 1)
            for n in range(4, 20):
                name = CH[n]
                if name.startswith("mod"):
                    mod_rows(name, n)
                    if name == "mod8":
                        cumulate()
                    continue
                w = take_chunk(n)
                if name.startswith("mqk"):
                    for m in range(4):
                        q = Q[f"{name}_{m}"]
                        bank_free(q)
                        for k in range(KD):
                            last = pe.matmul(psum[:, q % BANKS, 0:NTOK], w[:, k, 128 * m:128 * m + 128], hT[:, k, :],
                                             start=(k == 0), stop=(k == KD - 1))
                        if m == 3:
                            last.then_inc(used[n % 4], 1)
                            pe.wait_ge(used[n % 4], n // 4 + 1)
                            pe.nop().then_inc(S("projected"), 1)
                        else:
                            last.then_inc(S("projected"), 1)
                else:
                    for t in range(NT):
                        q = Q[f"{name}_{t}"]
                        bank_free(q)
                        for k in range(KD):
                            if t < 2:
                                last = pe.matmul(psum[:, q % BANKS, :], hT[:, k, tok(t)], w[:, k, :],
                                                 start=(k == 0), stop=(k == KD - 1))
                            else:
                                for u in range(2):
                                    last = pe.matmul(psum[64 * u:64 * u + 64, q % BANKS, 0:256], hT[:, k, tok(t)],
                                                     w[:, k, 256 * u:256 * u + 256], start=(k == 0),
                                                     stop=(k == KD - 1))
                        if t == 2:
                            last.then_inc(used[n % 4], 1)
                            pe.wait_ge(used[n % 4], n // 4 + 1)
                            pe.nop().then_inc(S("projected"), 1)
                        else:
                            last.then_inc(S("projected"), 1)
                        if (name, t) in SPREADS:
                            spread(*SPREADS[name, t])
                if name == "mqk1":
                    q = Q["gates"]
                    bank_free(q)
                    pe.wait_ge(S("small_in"), 16 * SMALL)
                    for k in range(KD):
                        last = pe.matmul(psum[0:8, q % BANKS, 0:NTOK], wg[:, k, :], hT[:, k, :],
                                         start=(k == 0), stop=(k == KD - 1))
                    last.then_inc(S("projected"), 1)
                    q = Q["gatesT"]
                    bank_free(q)
                    pe.wait_ge(S("evacuated"), Q["gates"] + 1)
                    for t in range(NT):
                        last = pe.transpose(psum[0:ROWS[t], q % BANKS, 8 * t:8 * t + 8], lgTm[0:8, tok(t)], ident[0:8, 0:8])
                    last.then_inc(S("projected"), 1)
                if name == "mv":
                    pe.wait_ge(S("qk_ready"), 1)
                    for t in range(NT):
                        q = Q[f"km{t}"]
                        bank_free(q)
                        for h in range(H):
                            last = pe.transpose(psum[0:ROWS[t], q % BANKS, 128 * h:128 * h + 128],
                                                qkT[:, H + h, tok(t)], ident)
                        last.then_inc(S("projected"), 1)
                    pe.wait_ge(S("cbuf_ready"), 1)
                    for u in range(2):
                        q = Q[f"conv{u}"]
                        bank_free(q)
                        for k in range(4):
                            last = pe.transpose(psum[0:27, q % BANKS, 128 * k:128 * k + 128], cbuf[:, 4 * u + k, :], ident)
                        last.then_inc(S("projected"), 1)
                if name == "rv":
                    for h in range(2 * H):
                        src = (rq, rk)[h // H]
                        pe.wait_ge(S("rotated"), h // H + 1)
                        q = Q[f"rT{h}"]
                        bank_free(q)
                        for t in range(NT):
                            last = pe.transpose(psum[:, q % BANKS, tok(t)],
                                                src[0:ROWS[t], t, 128 * (h % H):128 * (h % H) + 128],
                                                ident[0:ROWS[t], 0:ROWS[t]])
                        last.then_inc(S("projected"), 1)
            for n in (6, 7, 8, 9):
                mod_transposed(n)
            pe.wait_ge(S("evacuated"), NQ)

            pe.wait_ge(S("W_in"), NT)
            def score_bank(g):
                return 0 if g % 2 == 0 else 7

            def scores(g):
                kind, t = GROUPS[g]
                n = ROWS[t]
                src = qkT if kind else rT
                if g >= 2:
                    pe.wait_ge(S("sT_ready"), g - 1)
                for h in range(H):
                    last = pe.matmul(psum[0:n, score_bank(g), n * h:n * h + n], src[:, H + h, tok(t)],
                                     src[:, h, tok(t)], start=True, stop=True)
                last.then_inc(S("scored"), 1)

            scores(0)
            for g, (kind, t) in enumerate(GROUPS):
                n = ROWS[t]
                w = HD + kind
                src = qkT if kind else rT
                kt = km if kind else rk
                if g + 1 < len(GROUPS):
                    scores(g + 1)
                pe.wait_ge(S("sT_ready"), g + 1)
                pe.wait_ge(S("keys_ready"), 1 + kind)
                if g:
                    pe.wait_ge(S("combined"), g)
                for h in range(H):
                    v = vaug[0:n, t, h, :] if kind else rv[0:n, t, 128 * h:128 * h + 128]
                    last = pe.matmul(psum[0:n, 1 + h // 2, 129 * (h % 2):129 * (h % 2) + w], sT[0:n, h, 0:n], v,
                                     start=True, stop=True)
                last.then_inc(S("intra_done"), 1)
                if t < 2:
                    if t == 1:
                        pe.wait_ge(S("carried"), kind + 1)
                        for h in range(H):
                            last = pe.matmul(psum[0:n, 3 + h // 2, 129 * (h % 2):129 * (h % 2) + w],
                                             src[:, h, tok(t)], Cst[:, kind, h, 0:w], start=True, stop=True)
                        last.then_inc(S("inter_done"), 1)
                    if g:
                        pe.wait_ge(S("carried"), g)
                    for h in range(H):
                        v = vaug[0:n, t, h, :] if kind else rv[0:n, t, 128 * h:128 * h + 128]
                        last = pe.matmul(psum[:, 5 + h // 2, 129 * (h % 2):129 * (h % 2) + w],
                                         kt[0:n, t, 128 * h:128 * h + 128], v, start=True, stop=True)
                    last.then_inc(S("state_done"), 1)
                else:
                    for h in range(H):
                        i = kind * H + h
                        pe.wait_ge(S(f"S0_in{i}"), 16)
                        if kind:
                            pe.wait_ge(S("ncol_ready"), h + 1)
                        pe.wait_ge(S("qmask_ready"), i + 1)
                        for b in range(NSEQ):
                            last = pe.matmul(psum[0:64, 3 + h // 2, 129 * (h % 2):129 * (h % 2) + w],
                                             QMF[:, i % 2, 64 * b:64 * b + 64], S0(i)[:, b, 0:w],
                                             start=(b == 0), stop=(b == NSEQ - 1))
                        last.then_inc(S("inter_done"), 1)
                        pe.wait_ge(S("vmask_ready"), i + 1)
                        if i == 0:
                            pe.wait_ge(S("carried"), 4)
                        else:
                            pe.wait_ge(S("carriedS"), i)
                        for u in range(2):
                            last = pe.matmul(psum[:, 5 + u, :], kt[0:64, 2, 128 * h:128 * h + 128],
                                             vmask(i)[0:64, 4 * u:4 * u + 4, :].rearrange("p b e -> p (b e)"),
                                             start=True, stop=True)
                        if kind:
                            last = pe.matmul(psum[:, 0, NSEQ * h:NSEQ * h + NSEQ], km[0:64, 2, 128 * h:128 * h + 128],
                                             K("seqmask")[0:64, :], start=True, stop=True)
                        last.then_inc(S("stateS_done"), 1)
            pe.wait_ge(S("carriedS"), 2 * H)
            pe.transpose(psum[0:32, 0, 0:128], nT[:, 1, :], ident)
            pe.transpose(psum[0:4, 0, 128:256], Cst[:, 1, :, HD], ident).then_inc(S("n_rows"), 1)

            def turn_mixed(k, i):
                y = (rg, mo)[k // H]
                if i >= 6:
                    pe.wait_ge(S("evac2"), i - 5)
                for t in range(NT):
                    last = pe.transpose(psum[:, i % 6, tok(t)], y[0:ROWS[t], t, 128 * (k % H):128 * (k % H) + 128],
                                        ident[0:ROWS[t], 0:ROWS[t]])
                last.then_inc(S("proj2"), 1)

            def gate_rows(i0, n0):
                i = i0
                for t in range(NT):
                    for n in range(2):
                        if i >= 6:
                            pe.wait_ge(S("evac2"), i - 5)
                        for u in range(4):
                            last = pe.matmul(psum[0:ROWS[t], i % 6, 128 * u:128 * u + 128], sel[:, u, tok(t)],
                                             modr[:, n0 + n, :], start=True, stop=True)
                        last.then_inc(S("proj2"), 1)
                        i += 1

            pe.wait_ge(S("y_ready"), 5)
            pe.wait_ge(S("combined"), 6)
            pe.wait_ge(S("n_copied"), 1)
            for k in range(EARLY):
                turn_mixed(k, k)
            pe.wait_ge(S("sel_in"), 16)
            gate_rows(EARLY, 4)
            pe.wait_ge(S("y_ready"), 6)
            for k in range(EARLY, KD):
                turn_mixed(k, k + 6)
            pe.wait_ge(S("evac2"), KD + 6)
            for t in range(NT):
                for u in range(2):
                    i = 2 * t + u
                    w = take_chunk(20 + u)
                    if i >= 2:
                        pe.wait_ge(S("residual"), i - 1)
                    for k in range(KD):
                        if t < 2:
                            last = pe.matmul(psum[:, 6 + u, :], hT[:, k, tok(t)], w[:, k, :],
                                             start=(k == 0), stop=(k == KD - 1))
                            continue
                        for v in range(2):
                            last = pe.matmul(psum[64 * v:64 * v + 64, 6 + u, 0:256], hT[:, k, tok(t)],
                                             w[:, k, 256 * v:256 * v + 256], start=(k == 0), stop=(k == KD - 1))
                    last.then_inc(S("outproj"), 1)
            pe.wait_ge(S("outproj"), 6)
            pe.nop().then_inc(used[0], 1)
            pe.nop().then_inc(used[1], 1)
            gate_rows(KD + 6, 10)
            pe.wait_ge(S("xn2_ready"), 3)
            i = KD + 12
            for k in range(KD):
                pe.wait_ge(S("evac2"), i - 5)
                for t in range(NT):
                    last = pe.transpose(psum[:, i % 6, tok(t)], yfin[0:ROWS[t], t, 128 * k:128 * k + 128],
                                        ident[0:ROWS[t], 0:ROWS[t]])
                last.then_inc(S("proj2"), 1)
                i += 1
            pe.wait_ge(S("h2_ready"), 1)
            for k in range(KD):
                last = pe.matmul(psum[0:32, 6, 0:NTOK], wr[:, k, :], hT[:, k, :], start=(k == 0), stop=(k == KD - 1))
            last.then_inc(S("routerT"), 1)
            for t in range(NT):
                pe.wait_ge(S("evac2"), KD * 2 + 12)
                if t == 2:
                    pe.wait_ge(S("rest0"), 1)
                for k in range(KD):
                    b = 2 * (t % 2) + k // 4
                    last = pe.transpose(psum[0:ROWS[t], b, 128 * (k % 4):128 * (k % 4) + 128], hT[:, k, tok(t)], ident)
                last.then_inc(S("h2_rows"), 1)
            pe.wait_ge(S("lgT_ready"), 1)
            for t in range(NT):
                last = pe.transpose(psum[0:ROWS[t], 7, 32 * t:32 * t + 32], lgT[0:32, tok(t)], ident[0:32, 0:32])
            last.then_inc(S("logits"), 1)
            pe.wait_ge(S("route_ready"), 1)
            for t in range(NT):
                n = ROWS[t]
                for s in range(t):
                    pe.matmul(psum[0:n, 6, 32 * t:32 * t + 32], ones[:, 0:n], route[:, s, :], start=(s == 0), stop=False)
                pe.matmul(psum[0:n, 6, 32 * t:32 * t + 32], K("tri")[0:n, 0:n], route[0:n, t, :],
                          start=(t == 0), stop=True)
            for s in range(NT):
                last = pe.matmul(psum[:, 6, 96:128], ones[0:ROWS[s], :], route[0:ROWS[s], s, :], start=(s == 0),
                                 stop=(s == NT - 1))
            last.then_inc(S("places"), 1)

            def gather(i, count):
                def products(slots):
                    pe.wait_ge(S("P_ready"), i + 1)
                    for k in range(KD):
                        for part in range(3):
                            for t in range(NT):
                                last = pe.matmul(psum[:, 4 + k // 4, 128 * (k % 4):128 * (k % 4) + slots],
                                                 h2p[:, part, t, 128 * k:128 * k + 128], P[:, t, 0:slots],
                                                 start=(part == 0 and t == 0), stop=(part == 2 and t == NT - 1))
                    last.then_inc(S("gathered"), 1)
                by_size(pe, count, products)

            def up_products(slots, weights):
                if slots == 32:
                    w = weights.rearrange("p (l n) -> p l n", l=2)
                    return [(psum[32 * q:32 * q + 32, 0, :], w[:, :, 256 * q:256 * q + 256]) for q in range(4)]
                if slots == 64:
                    return [(psum[64 * q:64 * q + 64, lin, :], weights[:, D * lin + 512 * q:D * lin + 512 * q + 512])
                            for lin in range(2) for q in range(2)]
                return [(psum[:, b, :], weights[:, 512 * b:512 * b + 512]) for b in range(4)]

            def up(it, slots):
                for c in range(4):
                    pe.wait_ge(loaded[c], 16 * (it + USES[c] + 1))
                    w = at(c * SLOT, 2, 2 * D)
                    for j in range(2):
                        for out, moving in up_products(slots, w[:, j, :]):
                            last = pe.matmul(out, xg[:, 2 * c + j, 0:slots], moving,
                                             start=(c == 0 and j == 0), stop=False)
                    last.then_inc(used[c], 1)
                pe.wait_ge(S("bsel_ready"), it + 1)
                for out, moving in up_products(slots, bparts[:, 0:2 * D]):
                    last = pe.matmul(out, bsel[:, 0:slots], moving, start=False, stop=True)
                last.then_inc(S("up_done"), 1)

            def turn_activations(it, slots):
                pe.wait_ge(S("act_ready"), it + 1)
                for j in range(KD * slots // 128):
                    last = pe.transpose(flat(0, D)[:, 128 * j:128 * j + 128],
                                        gt_.rearrange("p u n -> p (u n)")[:, 128 * j:128 * j + 128], ident)
                last.then_inc(S("act_turned"), 1)

            def down(it, slots):
                tiles = 128 // slots
                pieces = KD // tiles
                for u in range(2):
                    pe.matmul(psum[0:slots, 2 + u, :], bsel[:, 0:slots],
                              bparts[:, 2 * D + 512 * u:2 * D + 512 * u + 512], start=True, stop=False)
                pe.wait_ge(S("actT_ready"), it + 1)
                for c in (4, 5):
                    pe.wait_ge(loaded[c], 16 * (it + USES[c] + 1))
                last = [None, None]
                for j in range(pieces):
                    for u in range(2):
                        for q in range(tiles):
                            piece = q * pieces + j
                            c = piece // 4
                            last[c] = pe.matmul(psum[slots * q:slots * q + slots, 2 + u, :],
                                                actT[:, j, slots * q:slots * q + slots],
                                                at((4 + c) * SLOT, 4, D)[:, piece % 4, 512 * u:512 * u + 512],
                                                start=(j == 0 and q > 0), stop=(j == pieces - 1))
                last[0].then_inc(used[4], 1)
                last[1].then_inc(used[5], 1)

            def scatter(it, t):
                if t < 2:
                    for u in range(2):
                        last = pe.matmul(psum[:, 6 - 2 * t + u, :], G[:, tok(t)], yd[:, u, :], start=True, stop=True)
                else:
                    for u in range(2):
                        last = pe.matmul(psum[64 * u:64 * u + 64, 6, :], G[:, tok(t)], yd[:, u, :],
                                         start=True, stop=True)
                last.then_inc(S("scattered"), 1)

            def expert(r, e, it, count, count_next):
                ig = r * (NE + 1) + e
                pe.wait_ge(S("xg_ready"), ig + 1)
                pe.wait_ge(S("y_copied"), it + 1)
                by_size(pe, count, lambda slots: up(it, slots))
                gather(ig + 1, count_next)
                pe.wait_ge(S("G_ready"), it + 1)
                pe.wait_ge(S("added"), 3 * it + 1)
                scatter(it, 0)
                pe.wait_ge(S("xg_ready"), ig + 2)
                scatter(it, 1)
                by_size(pe, count, lambda slots: turn_activations(it, slots))
                pe.wait_ge(S("Pg_ready"), it + 1)
                pe.wait_ge(S("added"), 3 * it + 2)
                for t in range(NT):
                    n = ROWS[t]
                    last = pe.transpose(psum[:, 7, tok(t)], Pg[0:n, t, :], ident[0:n, 0:n])
                last.then_inc(S("Pg_turned"), 1)
                scatter(it, 2)
                pe.wait_ge(S("added"), 3 * it + 3)
                by_size(pe, count, lambda slots: down(it, slots))

            def last_scatter(its):
                pe.wait_ge(S("G_ready"), its + 1)
                pe.wait_ge(S("y_copied"), its + 1)
                pe.wait_ge(S("added"), 3 * its + 1)
                for t in range(NT):
                    if t == 2:
                        pe.wait_ge(S("added"), 3 * its + 2)
                    scatter(its, t)

            for part in range(3):
                pe.wait_ge(S(f"part{part}"), NT)
            gather(0, None)
            with pe.Fori(0, NE) as e:
                count = pe.value_load(counts_i[0:1, bass.ds(e, 1)], min_val=0, max_val=NTOK)
                count_next = pe.value_load(counts_i[0:1, bass.ds(e + 1, 1)], min_val=0, max_val=NTOK)
                expert(0, e, e, count, count_next)
            most = pe.value_load(counts_i[0:1, NE:NE + 1], min_val=0, max_val=NTOK)
            with pe.If(most > BIG_BLOCK):
                with pe.Fori(1, ROUNDS) as r:
                    gather(r * (NE + 1), None)
                    with pe.Fori(0, NE) as e:
                        expert(r, e, r * NE + e, None, None)
                last_scatter(NE * ROUNDS)
            with pe.Else():
                last_scatter(NE)

        @block.scalar
        def _(act):
            for dst, src in ((prow[0:4, :], a["w_conv"][0]), (prow[4:5, :], a["b_conv"]),
                             (prow[5:6, :], a["g_mix"]), (prow[6:7, :], a["g_ffn"]),
                             (prow[7:31, :], a["state_conv"][0].rearrange("b j n -> (b j) n"))):
                act.dma_start(dst, src).then_inc(S("params_in"), 16)
            act.dma_start(nrow[0:32, :], a["state_mlstm_n"][0].rearrange("b h d -> (b h) d")).then_inc(S("nstate_in"), 16)
            act.wait_ge(S("c_in"), 32)
            act.activation(crow[0:9, :], crow[0:9, :], ACT.Silu).then_inc(S("c_silu"), 1)
            def bank(q, n=128):
                return psum[0:n, q % BANKS, :]

            def evac(name, pairs):
                act.wait_ge(S("projected"), Q[name] + 1)
                for dst, src in pairs[:-1]:
                    act.copy(dst, src)
                act.copy(*pairs[-1]).then_inc(S("evacuated"), 1)

            def bq(name):
                return Q[name] % BANKS

            act.wait_ge(S("zeroed"), 1)
            evac("c", [(cT[:, :, 0:9], psum[:, 0, 0:256].rearrange("p (k c) -> p k c", k=KD)[:, :, 0:9])])
            for t in range(4):
                src = a["b_mod"][0].rearrange("(n t j) -> t n j", t=4, j=128)[t]
                act.dma_start(bmod[32 * t:32 * t + 32, :, :], src.partition_broadcast(32)).then_inc(S("bmod_in"), 16)
            act.dma_start(wg[:, :, :], a["w_in"][0][:, 4096:4104].rearrange("(k p) n -> p k n", p=128)).then_inc(S("small_in"), 16)
            act.dma_start(igf[:, 0:4], a["b_igate"][0].partition_broadcast(128)).then_inc(S("small_in"), 16)
            act.dma_start(igf[:, 4:8], a["b_fgate"][0].partition_broadcast(128)).then_inc(S("small_in"), 16)
            act.dma_start(wr[:, :, :], a["w_router"][0].rearrange("(k p) n -> p k n", p=128)).then_inc(S("small_in"), 16)
            act.dma_start(brout, a["b_router"][0].partition_broadcast(128)).then_inc(S("small_in"), 16)
            act.dma_start(m0all[:, :, :], a["state_mlstm_m"][0].partition_broadcast(128)).then_inc(S("small_in"), 16)
            for b in range(NSEQ):
                act.dma_start(m0tok[TS * b:TS * b + TS, :], a["state_mlstm_m"][0][b].partition_broadcast(TS)).then_inc(S("small_in"), 16)
            def evac_mod(n):
                evac(f"mod{n}", [(modr[:, n, :], psum[:, bq(f"mod{n}"), 0:128])])

            def evac_modT(n):
                src = psum[:, bq(f"modT{n}"), 0:128].rearrange("p (t c) -> p t c", t=4)[:, :, 0:9]
                evac(f"modT{n}", [(modT[:, 4 * n:4 * n + 4, :], src)])

            for n in range(3):
                evac_mod(n)
            act.wait_ge(S("x_in"), 32)
            junk = at(o5, D)
            for t in range(NT):
                if t:
                    act.wait_ge(S("squares"), t)
                act.activation(junk[0:ROWS[t], :], xin[0:ROWS[t], t, :], ACT.Square,
                               accum_out=ss[0:ROWS[t], t:t + 1]).then_inc(S("squares"), 1)
            evac_mod(3)
            for n in range(4):
                evac_modT(n)
            b = bq("par")
            evac("par", [(parT[:, :, 0:31], psum[:, b, 0:248].rearrange("p (k c) -> p k c", k=KD))])
            evac("nstate", [(nT[:, 0, :], psum[:, bq("nstate"), 0:32])])
            for k in range(KD):
                evac(f"xnT{k}", [(xnT[:, k, :], psum[:, bq(f"xnT{k}"), 0:NTOK])])

            def log_sigmoid():
                act.wait_ge(S("fabs_ready"), 1)
                fa = gt["fabs"].rearrange("p t h -> p (t h)")
                act.activation(fa, fa, ACT.Exp, scale=-1.0).then_inc(S("fexp"), 1)
                act.wait_ge(S("fabs_ready"), 2)
                act.activation(fa, fa, ACT.Ln).then_inc(S("fexp"), 1)

            def decays(t):
                n = ROWS[t]
                act.wait_ge(S("W_in"), t + 1)
                tb = square_view(tmpB, n)
                for h in range(H):
                    last = act.activation(Wm[0:n, t, h, 0:n], tb[:, h, :], ACT.Exp, bias=gt["g"][0:n, t, h:h + 1])
                last.then_inc(S("W_done"), 1)

            DST = {"rq": rq, "rk": rk, "rv": rv, "rg": rg, "mo": mo}
            for n in range(4, 20):
                name = CH[n]
                if name.startswith("mod"):
                    evac_mod(int(name[3:]))
                elif name.startswith("mqk"):
                    for m in range(4):
                        k = 4 * int(name[3:]) + m
                        p = psum[:, bq(f"{name}_{m}"), :]
                        evac(f"{name}_{m}", [(xpp[:, k, 3:], p[:, 0:SEQ]),
                                             (xps[:, k, :, 3:], p[:, SEQ:NTOK].rearrange("p (b t) -> p b t", b=NSEQ))])
                else:
                    for t in range(NT):
                        b = bq(f"{name}_{t}")
                        if name == "mv":
                            def dst(n_, c0, c1):
                                return vaug[0:n_, t, c0 // 128:c1 // 128, 0:128]
                        else:
                            def dst(n_, c0, c1):
                                return DST[name][0:n_, t, c0:c1]
                        if t < 2:
                            src = psum[:, b, :]
                            if name == "mv":
                                src = src.rearrange("p (h e) -> p h e", h=4)
                            evac(f"{name}_{t}", [(dst(128, 0, 512), src)])
                        else:
                            pairs = []
                            for u in range(2):
                                src = psum[64 * u:64 * u + 64, b, 0:256]
                                if name == "mv":
                                    src = src.rearrange("p (h e) -> p h e", h=2)
                                pairs.append((dst(64, 256 * u, 256 * u + 256), src))
                            evac(f"{name}_{t}", pairs)
                if name == "mqk1":
                    evac("gates", [(lgTm[0:8, :], psum[0:8, bq("gates"), 0:NTOK])])
                    b = bq("gatesT")
                    evac("gatesT", [(gtok[:, 0:2, :], psum[:, b, 0:16].rearrange("p (t c) -> p t c", t=2)),
                                    (gtok[0:64, 2, :], psum[0:64, b, 16:24])])
                if name == "mv":
                    act.wait_ge(S("conv_done"), 1)
                    act.activation(qkT.rearrange("p k t -> p (k t)"), qkT.rearrange("p k t -> p (k t)"),
                                   ACT.Silu).then_inc(S("qk_ready"), 1)
                    for t in range(NT):
                        evac(f"km{t}", [(km[0:ROWS[t], t, :], bank(Q[f"km{t}"], ROWS[t]))])
                    for u in range(2):
                        evac(f"conv{u}", [(convrow[0:27, 512 * u:512 * u + 512], bank(Q[f"conv{u}"], 27))])
                    act.wait_ge(S("evacuated"), Q["conv1"] + 1)
                    act.dma_start(a["conv_p"][0, 0], convrow[0:3, :]).then_inc(S("conv_out"), 16)
                    act.dma_start(a["conv_s"][0].rearrange("b j n -> (b j) n"), convrow[3:27, :]).then_inc(S("conv_out"), 16)
                    log_sigmoid()
                if name == "rv":
                    for h in range(2 * H):
                        evac(f"rT{h}", [(rT[:, h, :], psum[:, bq(f"rT{h}"), 0:NTOK])])
                    decays(0)
                if name == "mo":
                    act.wait_ge(S("evacuated"), Q["mo_2"] + 1)
                    for t in range(NT):
                        last = act.activation(mo[0:ROWS[t], t, :], mo[0:ROWS[t], t, :], ACT.Sigmoid)
                    last.then_inc(S("gate_act"), 1)
                    decays(1)
                if name == "rg":
                    act.wait_ge(S("evacuated"), Q["rg_2"] + 1)
                    for t in range(NT):
                        last = act.activation(rg[0:ROWS[t], t, :], rg[0:ROWS[t], t, :], ACT.Silu)
                    last.then_inc(S("gate_act"), 1)
                    decays(2)
            for n in (6, 7, 8, 9):
                evac_modT(n)

            act.wait_ge(S("exps_in"), 1)
            for v in (gt["wint"].rearrange("p t h -> p (t h)"), gt["expm"].rearrange("p t h -> p (t h)"),
                      cdec[:, 1, :]):
                act.activation(v, v, ACT.Exp)
            act.activation(cdec[:, 0, 0:4], cdec[:, 0, 0:4], ACT.Exp).then_inc(S("exps_done"), 1)
            act.dma_start(a["m_p"][0], gt["mt"][127:128, 1, :]).then_inc(S("state_out"), 16)
            act.dma_start(a["m_s"][0], gt["mt"][TS - 1:64:TS, 2, :]).then_inc(S("state_out"), 16)
            act.wait_ge(S("carried"), 3)
            act.dma_start(a["ret_p"][0, 0].rearrange("h d e -> d h e"), Cst[:, 0, :, 0:HD]).then_inc(S("state_out"), 16)
            act.wait_ge(S("carried"), 4)
            act.dma_start(a["c_p"][0, 0].rearrange("h d e -> d h e"), Cst[:, 1, :, 0:HD]).then_inc(S("state_out"), 16)
            for i in range(2 * H):
                act.wait_ge(S("carriedS"), i + 1)
                dst = a["c_s"] if i >= H else a["ret_s"]
                act.dma_start(dst[0][:, i % H].rearrange("b d e -> d b e"), S0(i)[:, :, 0:HD])\
                   .then_inc(S("S0_out"), 16)
            act.wait_ge(S("n_rows"), 1)
            act.copy(tmpB[0:32, 0, :], psum[0:32, 0, 0:128])
            act.copy(tmpB[0:4, 1, :], psum[0:4, 0, 128:256]).then_inc(S("n_copied"), 1)
            act.wait_ge(S("n_copied"), 1)
            act.dma_start(a["n_s"][0].rearrange("b h d -> (b h) d"), tmpB[0:32, 0, :]).then_inc(S("state_out"), 16)
            act.dma_start(a["n_p"][0, 0], tmpB[0:4, 1, :]).then_inc(S("state_out"), 16)
            act.wait_ge(S("stateS_done"), 8)
            act.wait_ge(S("qmask_ready"), 8)
            act.dma_start(sel.rearrange("p u t -> p (u t)"), a["selectors"]).then_inc(S("sel_in"), 16)
            act.dma_start(x2[:, 0:2, :], a["x_prompt"][0].rearrange("(t p) d -> p t d", p=128)).then_inc(S("x2_in"), 16)
            act.dma_start(x2[0:64, 2, :], a["x_sample"].rearrange("b t d -> (b t) d")).then_inc(S("x2_in"), 16)

            def evac2(i, dst, n, cols=512):
                act.wait_ge(S("proj2"), i + 1)
                act.copy(dst, psum[0:n, i % 6, 0:cols]).then_inc(S("evac2"), 1)

            for k in range(EARLY):
                evac2(k, hT[:, k, :], 128, NTOK)
            i = EARLY
            for t in range(NT):
                for u in range(2):
                    evac2(i, gateA[0:ROWS[t], t, 512 * u:512 * u + 512], ROWS[t])
                    i += 1
            act.wait_ge(S("y_ready"), len(GROUPS))
            for k in range(EARLY, KD):
                evac2(i, hT[:, k, :], 128, NTOK)
                i += 1
            for t in range(NT):
                act.wait_ge(S("residual"), 2 * t + 2)
                act.wait_ge(S("squares"), 3 + t)
                act.activation(yd.rearrange("p u n -> p (u n)")[0:ROWS[t], :], x2[0:ROWS[t], t, :], ACT.Square,
                               accum_out=ss[0:ROWS[t], 3 + t:4 + t]).then_inc(S("squares"), 1)
            for t in range(NT):
                for u in range(2):
                    evac2(i, gateF[0:ROWS[t], t, 512 * u:512 * u + 512], ROWS[t])
                    i += 1
            for k in range(KD):
                evac2(i, xnT2[:, k, :], 128, NTOK)
                i += 1
            act.wait_ge(S("routerT"), 1)
            act.copy(lgT[0:32, :], psum[0:32, 6, 0:NTOK]).then_inc(S("lgT_ready"), 1)
            for t, part in SPLIT:
                n = ROWS[t]
                if part == 0:
                    act.wait_ge(S("h2_rows"), t + 1)
                    src = flat(2 * (t % 2), D)[0:n]
                else:
                    act.wait_ge(S(f"rest{part - 1}"), t + 1)
                    src = yfin[0:n, t, :]
                act.copy(h2p[0:n, part, t, :], src).then_inc(S(f"part{part}"), 1)
            act.wait_ge(S("softmax_in"), 1)
            for t in range(NT):
                n = ROWS[t]
                last = act.activation(pexp[0:n, t, :], logit[0:n, t, :], ACT.Exp, bias=nmax[0:n, t:t + 1])
            last.then_inc(S("softmax_exp"), 1)

            def copy_gathered(i, count):
                def copy(slots):
                    act.wait_ge(S("gathered"), i + 1)
                    act.copy(xg[:, :, 0:slots], flat(4, D).rearrange("p (k s) -> p k s", k=KD)[:, :, 0:slots])\
                       .then_inc(S("xg_ready"), 1)
                by_size(act, count, copy)

            def expert(r, e, it, count, count_next):
                ig = r * (NE + 1) + e

                def sigmoid(slots):
                    n = 8 * slots
                    act.wait_ge(S("gate_ready"), it + 1)
                    act.activation(sg.rearrange("p u n -> p (u n)")[:, 0:n], gt_.rearrange("p u n -> p (u n)")[:, 0:n],
                                   ACT.Sigmoid, scale=1.702).then_inc(S("sig_ready"), 1)

                def turned(slots):
                    n = 8 * slots
                    act.wait_ge(S("act_turned"), it + 1)
                    act.copy(actT.rearrange("p j s -> p (j s)")[:, 0:n], flat(0, n)).then_inc(S("actT_ready"), 1)

                by_size(act, count, sigmoid)
                copy_gathered(ig + 1, count_next)
                by_size(act, count, turned)
                act.wait_ge(S("Pg_turned"), it + 1)
                act.wait_ge(S("scattered"), 3 * it + 3)
                act.copy(G, psum[:, 7, 0:NTOK]).then_inc(S("G_ready"), 1)
                act.wait_ge(used[4], it + 1)
                act.wait_ge(used[5], it + 1)
                act.copy(yd.rearrange("p u n -> p (u n)"), flat(2, D)).then_inc(S("y_copied"), 1)

            act.wait_ge(S("P_zero"), 1)
            act.nop().then_inc(S("G_ready"), 1)
            act.nop().then_inc(S("y_copied"), 1)
            copy_gathered(0, None)
            with act.Fori(0, NE) as e:
                count = act.value_load(counts_i[0:1, bass.ds(e, 1)], min_val=0, max_val=NTOK)
                count_next = act.value_load(counts_i[0:1, bass.ds(e + 1, 1)], min_val=0, max_val=NTOK)
                expert(0, e, e, count, count_next)
            most = act.value_load(counts_i[0:1, NE:NE + 1], min_val=0, max_val=NTOK)
            with act.If(most > BIG_BLOCK):
                with act.Fori(1, ROUNDS) as r:
                    copy_gathered(r * (NE + 1), None)
                    with act.Fori(0, NE) as e:
                        expert(r, e, r * NE + e, None, None)
            with act.Else():
                act.nop()
            act.dma_start(gfin.rearrange("p u n -> p (u n)"), a["g_final"].partition_broadcast(128)).then_inc(S("gfin_in"), 16)
            for t in range(NT):
                act.wait_ge(S("x3_ready"), t + 1)
                act.wait_ge(S("squares"), 6 + t)
                act.activation(gt_.rearrange("p u n -> p (u n)")[0:ROWS[t], :], x2[0:ROWS[t], t, :], ACT.Square,
                               accum_out=ss[0:ROWS[t], t:t + 1]).then_inc(S("squares"), 1)
            act.wait_ge(S("y_final"), 2)
            act.dma_start(a["y_prompt"][0].rearrange("(t p) d -> p t d", p=128), x2[:, 0:2, :]).then_inc(S("y_out"), 16)
            act.wait_ge(S("y_final"), 3)
            act.dma_start(a["y_sample"].rearrange("b t d -> (b t) d"), x2[0:64, 2, :]).then_inc(S("y_out"), 16)
            act.wait_ge(S("y_out"), 32)
            act.wait_ge(S("state_out"), 16 * STORES)
            act.wait_ge(S("conv_out"), 32)

        @block.gpsimd
        def _(pool):
            step = chained(pool, "pool_step")
            pool.memset(cT, 0.0)
            pool.memset(halves, -0.5)
            pool.memset(ss, 1.0)
            for k in gt:
                pool.memset(gt[k], 0.0)
            pool.memset(gtok, 0.0)
            pool.memset(QMF, 0.0)
            pool.memset(xpp[:, :, 0:3], 0.0)
            pool.memset(cdec, 0.0)
            pool.memset(vaug[:, :, :, HD:HD + 1], 1.0).then_inc(S("zeroed"), 1)
            pool.wait_ge(S("zeroed"), 1)

            def rstd(out, src, scale):
                step(pool.tensor_scalar(out, src, scale, EPS, ALU.mult, ALU.add))
                return pool.tensor_tensor(out, out, halves[0:out.shape[0], 0:out.shape[1]], ALU.pow)


            def mod_bias(n):
                pool.wait_ge(S("evacuated"), Q[f"mod{n}"] + 1)
                pool.tensor_tensor(modr[:, n, :], modr[:, n, :], bmod[:, n, :], ALU.add).then_inc(S("mod_biased"), 1)

            pool.wait_ge(S("bmod_in"), 64)
            for n in range(3):
                mod_bias(n)
            pool.wait_ge(S("squares"), 3)
            rstd(rs[:, 0:3], ss[:, 0:3], 1.0 / D).then_inc(S("rstd_ready"), 1)
            mod_bias(3)
            pool.wait_ge(S("evacuated"), Q["par"] + 1)
            for k in range(KD):
                last = pool.tensor_copy(xps[:, k, :, 0:3], parT[:, k, 7:31].rearrange("p (b j) -> p b j", b=NSEQ))
            last.then_inc(S("xps_ready"), 1)
            mod_bias(4)
            mod_bias(5)
            pool.wait_ge(S("evacuated"), Q["mqk1_3"] + 1)
            pool.wait_ge(S("xps_ready"), 1)
            pool.tensor_copy(cbuf[:, :, 0:3], xpp[:, :, SEQ:SEQ + 3])
            for k in range(KD):
                last = pool.tensor_copy(cbuf[:, k, 3:27].rearrange("p (b j) -> p b j", b=NSEQ), xps[:, k, :, TS:TS + 3])
            last.then_inc(S("cbuf_ready"), 1)
            pool.wait_ge(S("cbuf_ready"), 1)
            pool.wait_ge(S("conv_done"), 1)
            pool.dma_start(gnorm[:, 0, :], a["g_ret"][0].rearrange("h d -> (h d)").partition_broadcast(128)).then_inc(S("gnorm_in"), 16)
            pool.dma_start(gnorm[:, 1, :], a["g_mlstm"][0].rearrange("h d -> (h d)").partition_broadcast(128)).then_inc(S("gnorm_in"), 16)
            for n in range(6, 10):
                mod_bias(n)
            pool.wait_ge(S("gnorm_in"), 32)

            def scale_gates(kind):
                z = (rg, mo)[kind]
                pool.wait_ge(S("gate_act"), 2 - kind)
                for t in range(NT):
                    n = ROWS[t]
                    last = pool.tensor_tensor(z[0:n, t, :], z[0:n, t, :], gnorm[0:n, kind, :], ALU.mult)
                return last

            step(scale_gates(1))
            mod_bias(10)
            pool.wait_ge(S("mod_biased"), 11)
            scale_gates(0).then_inc(S("gates_scaled"), 1)
            pool.wait_ge(S("gates_scaled"), 1)
            mod_bias(11)

            def mask_queries(i):
                q = (qkT if i >= H else rT)[:, i % H, SEQ:NTOK].rearrange("p (b t) -> p b t", b=NSEQ)
                pool.tensor_copy(QM[:, i % 2, :, 0:TS], q).then_inc(S("qmask_ready"), 1)

            def mask_values(i):
                h = i % H
                v = vaug[0:64, 2, h, 0:HD] if i >= H else rv[0:64, 2, 128 * h:128 * h + 128]
                pool.tensor_tensor(vmask(i)[0:64, :, :], v.unsqueeze(1).to_broadcast([64, NSEQ, HD]),
                                   K("seqmask")[0:64, :].unsqueeze(2).to_broadcast([64, NSEQ, HD]),
                                   ALU.mult).then_inc(S("vmask_ready"), 1)

            def head_rstd(g):
                pool.wait_ge(S("moments"), g + 1)
                n = ROWS[GROUPS[g][1]]
                rstd(hr[0:n, :], mv2[0:n, :, 1], 1.0).then_inc(S("head_rstd"), 1)

            pool.wait_ge(S("mod_biased"), 12)
            for g in range(3):
                head_rstd(g)
            pool.wait_ge(S("evacuated"), Q["rT7"] + 1)
            mask_queries(0)
            mask_queries(1)
            pool.wait_ge(S("conv_out"), 32)
            mask_values(0)
            head_rstd(3)
            for i in range(1, 2 * H):
                if i >= 2:
                    pool.wait_ge(S("stateS_done"), i - 1)
                mask_values(i)
                if i >= 2:
                    mask_queries(i)
                if i >= H:
                    pool.wait_ge(S(f"S0_in{i}"), 16)
                    pool.tensor_copy(S0(i)[:, :, HD:HD + 1],
                                     nT[:, 0, :].rearrange("p (b h) -> p b h", h=H)[:, :, i - H:i - H + 1])\
                        .then_inc(S("ncol_ready"), 1)
                if i == H:
                    head_rstd(4)
            head_rstd(5)
            pool.wait_ge(S("y_ready"), len(GROUPS))
            pool.wait_ge(S("state_out"), 16 * STORES)
            pool.wait_ge(S("S0_out"), 16 * 2 * H)
            for q in range(4):
                pool.dma_start(brows[32 * q:32 * q + 32, 0:2 * D], a["b_up"][0]).then_inc(S("brows_in"), 16)
                pool.dma_start(brows[32 * q:32 * q + 32, 2 * D:3 * D], a["b_down"][0]).then_inc(S("brows_in"), 16)
            pool.wait_ge(S("squares"), 6)
            rstd(rs[:, 0:3], ss[:, 3:6], 1.0 / D).then_inc(S("rstd_ready"), 1)
            pool.wait_ge(S("residual"), 6)
            pool.wait_ge(S("rstd_ready"), 2)
            step(pool.memset(h2p[64:128, :, 2, :], 0.0))
            pool.wait_ge(S("brows_in"), 16 * 8)
            pool.wait_ge(S("proj2"), KD + 12)
            step(pool.tensor_copy(bparts, brows))
            step(pool.tensor_tensor(brows[64:128, :], brows[64:128, :], bparts[64:128, :], ALU.subtract))
            pool.wait_ge(S("h2_rows"), NT)
            pool.memset(G, 0.0)
            pool.memset(yd, 0.0)
            pool.memset(P, 0.0).then_inc(S("P_zero"), 1)
            pool.wait_ge(S("P_zero"), 1)
            step(pool.tensor_copy(bparts[64:128, :], brows[64:128, :]))
            step(pool.tensor_tensor(brows[96:128, :], brows[96:128, :], bparts[96:128, :], ALU.subtract))
            pool.tensor_copy(bparts[96:128, :], brows[96:128, :]).then_inc(S("bias_split"), 1)
            pool.wait_ge(S("bias_split"), 1)

            def expert(r, e, it):
                pool.wait_ge(used[4], it + 1)
                pick_bias(e + 1)

            def pick_bias(e):
                col = bass.ds(e, 1) if not isinstance(e, int) else slice(e, e + 1)
                pool.tensor_copy(bsel, K("biasrow")[:, col].to_broadcast([128, 128])).then_inc(S("bsel_ready"), 1)

            pick_bias(0)
            with pool.Fori(0, NE) as e:
                expert(0, e, e)
            pool.wait_ge(S("counts_ready"), 1)
            most = pool.value_load(counts_i[0:1, NE:NE + 1], min_val=0, max_val=NTOK)
            with pool.If(most > BIG_BLOCK):
                with pool.Fori(1, ROUNDS) as r:
                    with pool.Fori(0, NE) as e:
                        expert(r, e, r * NE + e)
            with pool.Else():
                pool.nop()
            for t in range(NT):
                pool.wait_ge(S("squares"), 7 + t)
                n = ROWS[t]
                rstd(rs[0:n, t:t + 1], ss[0:n, t:t + 1], 1.0 / D).then_inc(S("rstd3"), 1)

        @block.vector
        def _(dve):
            step = chained(dve, "dve_step")
            TT, TSC, STT = dve.tensor_tensor, dve.tensor_scalar, dve.scalar_tensor_tensor

            dve.wait_ge(S("rstd_ready"), 1)
            for t in range(NT):
                TSC(xin[0:ROWS[t], t, :], xin[0:ROWS[t], t, :], rs[0:ROWS[t], t:t + 1], None, ALU.mult)\
                    .then_inc(S("xn_ready"), 1)

            def modulate(src, coef, n0, g_row, sem):
                step(STT(coef, modT[:, n0 + 8:n0 + 16, :], 1.0,
                         parT[:, :, g_row:g_row + 1].to_broadcast([128, KD, 9]), ALU.add, ALU.mult))
                for k in range(KD):
                    TSC(hT[:, k, 0:SEQ], src[:, k, 0:SEQ], coef[:, k, 0:1], modT[:, n0 + k, 0:1], ALU.mult, ALU.add)

                def seqs(v):
                    return v[:, :, SEQ:NTOK].rearrange("p k (b t) -> p k b t", b=NSEQ)

                def cols(v):
                    return v.unsqueeze(3).to_broadcast([128, KD, NSEQ, TS])
                step(TT(seqs(hT), seqs(src), cols(coef[:, :, 1:9]), ALU.mult))
                TT(seqs(hT), seqs(hT), cols(modT[:, n0:n0 + 8, 1:9]), ALU.add).then_inc(S(sem), 1)

            dve.wait_ge(S("evacuated"), Q[f"xnT{KD - 1}"] + 1)
            modulate(xnT, coefA, 0, 5, "h_ready")

            dve.wait_ge(S("evacuated"), Q["mqk1_3"] + 1)
            dve.wait_ge(S("xps_ready"), 1)
            for j in range(4):
                for k in range(KD):
                    wj = parT[:, k, j:j + 1]
                    outs = (qkT[:, k, 0:SEQ], qkT[:, k, SEQ:NTOK].rearrange("p (b t) -> p b t", b=NSEQ))
                    ins = (xpp[:, k, j:j + SEQ], xps[:, k, :, j:j + TS])
                    for y, x in zip(outs, ins):
                        if j == 0:
                            last = TSC(y, x, wj, parT[:, k, 4:5], ALU.mult, ALU.add)
                        else:
                            last = STT(y, x, wj, y, ALU.mult, ALU.add)
                if j < 3:
                    step(last)
                else:
                    last.then_inc(S("conv_done"), 1)

            dve.wait_ge(S("more_tables_in"), 16)
            ta = tmpA.rearrange("p h (u j) -> p h u j", u=2)
            tb = tmpB.rearrange("p h (u j) -> p h u j", u=2)
            for m, (name, z) in enumerate((("rq", rq), ("rk", rk))):
                for t in range(NT):
                    n = ROWS[t]
                    dve.wait_ge(S("evacuated"), Q[f"{name}_{t}"] + 1)
                    v = z[0:n, t, :].rearrange("p (h u j) -> p h u j", h=H, u=2)
                    cos = K("cos", NT, 64)[0:n, t, :]
                    sin = K("sin", NT, 64)[0:n, t, :].unsqueeze(1).to_broadcast([n, H, 64])
                    cosb = cos.unsqueeze(1).unsqueeze(1).to_broadcast([n, H, 2, 64])
                    TT(ta[0:n], v, cosb, ALU.mult)
                    TT(tb[0:n, :, 0, :], v[:, :, 1, :], sin, ALU.mult)
                    step(TT(tb[0:n, :, 1, :], v[:, :, 0, :], sin, ALU.mult))
                    TT(v[:, :, 0, :], ta[0:n, :, 0, :], tb[0:n, :, 0, :], ALU.subtract)
                    last = TT(v[:, :, 1, :], ta[0:n, :, 1, :], tb[0:n, :, 1, :], ALU.add)
                    if t < NT - 1:
                        step(last)
                last.then_inc(S("rotated"), 1)
                dve.wait_ge(S("rotated"), m + 1)

            dve.wait_ge(S("evacuated"), Q["gatesT"] + 1)
            dve.wait_ge(S("small_in"), 16 * SMALL)
            TT(gt["ipre"], gtok[:, :, 0:4], igf[:, 0:4].unsqueeze(1).to_broadcast([128, NT, H]), ALU.add)
            step(TT(gt["fpre"], gtok[:, :, 4:8], igf[:, 4:8].unsqueeze(1).to_broadcast([128, NT, H]), ALU.add))
            STT(gt["fabs"], gt["fpre"], -1.0, gt["fpre"], ALU.mult, ALU.max).then_inc(S("fabs_ready"), 1)
            dve.wait_ge(S("fexp"), 1)
            TSC(gt["fabs"], gt["fabs"], 1.0, None, ALU.add).then_inc(S("fabs_ready"), 1)
            dve.wait_ge(S("fexp"), 2)
            STT(gt["fpre"], gt["fpre"], 0.0, gt["fabs"], ALU.min, ALU.subtract).then_inc(S("logf_ready"), 1)

            b_, g_, M_ = gt["b"], gt["g"], gt["M"]
            dve.wait_ge(S("cumsum_done"), 1)
            dve.tensor_copy(b_[:, 0:2, :], psum[:, 6, 0:8].rearrange("p (t h) -> p t h", t=2))
            dve.tensor_copy(b_[0:64, 2, :], psum[0:64, 6, 8:12])
            step(dve.tensor_copy(gt["btot"][:, 0:2, :], psum[:, 6, 12:20].rearrange("p (t h) -> p t h", t=2)))
            step(TT(g_, gt["ipre"], b_, ALU.subtract))

            def diagonal(v, n):
                return TT(square_view(tmpA, n), ident[0:n, 0:n].unsqueeze(1).to_broadcast([n, H, n]),
                          v.unsqueeze(2).to_broadcast([n, H, n]), ALU.mult)

            for t in range(NT):
                n = ROWS[t]
                mask, maskT = (K("mask"), K("maskT")) if t < 2 else (K("maskS"), K("maskST"))
                diagonal(g_[0:n, t, :], n).then_inc(S("diag_ready"), 1)
                if t == 1:
                    TT(gt["mprev"][:, 1, :], gt["mlast"][:, 0, :], gt["btot"][:, 0, :], ALU.add)
                if t == 2:
                    dve.tensor_copy(gt["mprev"][0:64, 2, :], m0tok[0:64, :])
                dve.wait_ge(S("spread"), 2 * t + 1)
                if t:
                    dve.wait_ge(S("W_done"), t)
                tbv = square_view(tmpB, n)
                step(TT(tbv, psum[0:n, 6, 0:H * n].rearrange("p (h j) -> p h j", h=H),
                        mask[0:n, 0:n].unsqueeze(1).to_broadcast([n, H, n]), ALU.add))
                step(dve.reduce_max(M_[0:n, t, :], tbv, X))
                step(TT(M_[0:n, t, :], M_[0:n, t, :], gt["mprev"][0:n, t, :], ALU.max))
                TT(gt["mt"][0:n, t, :], b_[0:n, t, :], M_[0:n, t, :], ALU.add)
                diagonal(M_[0:n, t, :], n).then_inc(S("diag_ready"), 1)
                dve.wait_ge(S("spread"), 2 * t + 2)
                Mb = psum[:, 7, 0:H * n].rearrange("p (h j) -> p h j", h=H)
                if t < 2:
                    dve.tensor_copy(gt["mlast"][:, t, :].unsqueeze(2), Mb[:, :, n - 1:n])
                else:
                    dve.tensor_copy(mlS, Mb[:, :, TS - 1:n:TS])
                TT(tbv, maskT[0:n, 0:n].unsqueeze(1).to_broadcast([n, H, n]), Mb[0:n], ALU.subtract)\
                    .then_inc(S("W_in"), 1)
                dve.wait_ge(S("W_in"), t + 1)
            TT(gt["wint"], gt["mprev"], M_, ALU.subtract)
            TSC(gt["expm"], gt["mt"], -1.0, None, ALU.mult)
            TT(cdec[:, 0, 0:4], gt["mprev"][:, 1, :], gt["mlast"][:, 1, :], ALU.subtract)
            TT(cdec[:, 1, :].rearrange("p (b h) -> p b h", h=H), m0all, mlS.rearrange("p h b -> p b h"),
               ALU.subtract).then_inc(S("exps_in"), 1)
            dve.wait_ge(S("evacuated"), Q["rT7"] + 1)
            for t in range(NT):
                n = ROWS[t]
                v = rk[0:n, t, :].rearrange("p (h d) -> p h d", h=H)
                last = TT(v, v, K("kdec", NT, H)[0:n, t, :].unsqueeze(2).to_broadcast([n, H, HD]), ALU.mult)
            last.then_inc(S("keys_ready"), 1)
            dve.wait_ge(S("W_done"), NT)
            TSC(gt["wk"][:, 0:2, :].unsqueeze(3), Wm[:, 0:2, :, 127:128], SCALE, None, ALU.mult)
            step(dve.reduce_sum(gt["wk"][0:64, 2, :], Wm[0:64, 2, :, TS - 1:64:TS], X))
            step(TSC(gt["wk"][0:64, 2, :], gt["wk"][0:64, 2, :], SCALE, None, ALU.mult))
            for t in range(NT):
                n = ROWS[t]
                v = km[0:n, t, :].rearrange("p (h d) -> p h d", h=H)
                last = TT(v, v, gt["wk"][0:n, t, :].unsqueeze(2).to_broadcast([n, H, HD]), ALU.mult)
            last.then_inc(S("keys_ready"), 1)
            dve.wait_ge(S("exps_done"), 1)

            def pair_view(bank0, n, w):
                return psum[0:n, bank0:bank0 + 2, 0:258].rearrange("p b (h e) -> p b h e", h=2)[:, :, :, 0:w]

            def weigh_scores(g):
                kind, t = GROUPS[g]
                n = ROWS[t]
                w = HD + kind
                dve.wait_ge(S("scored"), g + 1)
                if g:
                    dve.wait_ge(S("intra_done"), g)
                bank = 0 if g % 2 == 0 else 7
                sc = psum[0:n, bank, 0:H * n].rearrange("p (h i) -> p h i", h=H)
                if kind:
                    STT(sT[0:n, :, 0:n], sc, SCALE, Wm[0:n, t, :, 0:n], ALU.mult, ALU.mult).then_inc(S("sT_ready"), 1)
                else:
                    dec = K("decT", H, 128) if t < 2 else K("decTS", H, 64)
                    TT(sT[0:n, :, 0:n], sc, dec[0:n], ALU.mult).then_inc(S("sT_ready"), 1)

            def carry(g):
                kind, t = GROUPS[g]
                n = ROWS[t]
                w = HD + kind
                def carry_prompt():
                    dve.wait_ge(S("state_done"), g + 1)
                    cs = Cst[:, kind].rearrange("p (a h) e -> p a h e", a=2)[:, :, :, 0:w]
                    if t == 0:
                        dve.tensor_copy(cs, pair_view(5, 128, w)).then_inc(S("carried"), 1)
                        return
                    dve.wait_ge(S("inter_done"), kind + 1)
                    for h in range(H):
                        dec = float(np.exp(lg[h] * np.float32(128))) if kind == 0 else cdec[:, 0, h:h + 1]
                        last = STT(Cst[:, kind, h, 0:w], Cst[:, kind, h, 0:w], dec,
                                   psum[:, 5 + h // 2, 129 * (h % 2):129 * (h % 2) + w], ALU.mult, ALU.add)
                    last.then_inc(S("carried"), 1)

                def carry_samples():
                    for h in range(H):
                        i = kind * H + h
                        dve.wait_ge(S("stateS_done"), i + 1)
                        ps = psum[:, 5:7, :].rearrange("p a (b e) -> p (a b) e", e=HD)
                        s0 = S0(i)[:, :, 0:HD]
                        if kind == 0:
                            dec = float(np.exp(lg[h] * np.float32(TS)))
                            last = STT(s0, s0, dec, ps, ALU.mult, ALU.add)
                        else:
                            for b in range(NSEQ):
                                STT(s0[:, b, :], s0[:, b, :], cdec[:, 1, H * b + h:H * b + h + 1], ps[:, b, :],
                                    ALU.mult, ALU.add)

                            def nh(k):
                                return nT[:, k, :].rearrange("p (b h) -> p b h", h=H)[:, :, h]
                            step(TT(nh(1), nh(0), cdec[:, 1, :].rearrange("p (b h) -> p b h", h=H)[:, :, h], ALU.mult))
                            last = TT(nh(1), nh(1), psum[:, 0, NSEQ * h:NSEQ * h + NSEQ], ALU.add)
                        last.then_inc(S("carriedS"), 1)

                carry_prompt() if t < 2 else carry_samples()

            def combine(g):
                kind, t = GROUPS[g]
                n = ROWS[t]
                w = HD + kind
                dve.wait_ge(S("intra_done"), g + 1)
                cv = comb[0:n].rearrange("p (a h) e -> p a h e", a=2)[:, :, :, 0:w]
                if t == 0:
                    dve.tensor_copy(cv, pair_view(1, n, w)).then_inc(S("combined"), 1)
                else:
                    dve.wait_ge(S("inter_done"), (kind + 1) if t == 1 else 2 + H * (kind + 1))
                    dec = gt["wint"][0:n, t, :] if kind else K("qdec", NT, H)[0:n, t, :]
                    step(TT(cv, pair_view(3, n, w), dec.rearrange("p (a h) -> p a h", a=2).unsqueeze(3)
                            .to_broadcast([n, 2, 2, w]), ALU.mult))
                    TT(cv, cv, pair_view(1, n, w), ALU.add).then_inc(S("combined"), 1)
                dve.wait_ge(S("combined"), g + 1)

            def norm_start(g):
                kind, t = GROUPS[g]
                n = ROWS[t]
                w = HD + kind
                y = comb[0:n, :, 0:HD]
                if kind:
                    den = comb[0:n, :, HD]
                    d = stat[0:n, 4:8]
                    step(STT(d, den, -1.0, den, ALU.mult, ALU.max))
                    step(TT(d, d, gt["expm"][0:n, t, :], ALU.max))
                    step(dve.reciprocal(d, d))
                    step(TT(y, y, d.unsqueeze(2).to_broadcast([n, H, HD]), ALU.mult))
                for h in range(H):
                    last = dve.bn_stats(stat[0:n, 16 + 6 * h:22 + 6 * h], comb[0:n, h, 0:HD])
                step(last)
                if g:
                    dve.wait_ge(S("head_rstd"), g)
                for h in range(H):
                    last = dve.bn_aggr(mv2[0:n, h, :], stat[0:n, 16 + 6 * h:22 + 6 * h])
                last.then_inc(S("moments"), 1)

            def norm_end(g):
                kind, t = GROUPS[g]
                n = ROWS[t]
                w = HD + kind
                dve.wait_ge(S("head_rstd"), g + 1)
                for h in range(H):
                    last = TSC(nrm[0:n, h, :], comb[0:n, h, 0:HD], mv2[0:n, h, 0:1], hr[0:n, h:h + 1],
                               ALU.subtract, ALU.mult)
                step(last)
                if g == 0:
                    dve.wait_ge(S("gates_scaled"), 1)
                z = (mo if kind else rg)[0:n, t, :].rearrange("p (h d) -> p h d", h=H)
                TT(z, nrm[0:n], z, ALU.mult).then_inc(S("y_ready"), 1)

            weigh_scores(0)
            carry(0)
            combine(0)
            for g in range(len(GROUPS)):
                more = g + 1 < len(GROUPS)
                samples = more and GROUPS[g + 1][1] == 2
                if more:
                    weigh_scores(g + 1)
                norm_start(g)
                if more and not samples:
                    carry(g + 1)
                norm_end(g)
                if samples:
                    carry(g + 1)
                if more:
                    combine(g + 1)

            dve.wait_ge(S("x2_in"), 32)
            dve.wait_ge(S("evac2"), KD + 6)
            for t in range(NT):
                n = ROWS[t]
                for u in range(2):
                    i = 2 * t + u
                    dve.wait_ge(S("outproj"), i + 1)
                    xs = x2[0:n, t, 512 * u:512 * u + 512]
                    ga = gateA[0:n, t, 512 * u:512 * u + 512]
                    if t < 2:
                        step(TT(ga, psum[0:n, 6 + u, :], ga, ALU.mult))
                    else:
                        for v in range(2):
                            gv = ga[:, 256 * v:256 * v + 256]
                            last = TT(gv, psum[64 * v:64 * v + 64, 6 + u, 0:256], gv, ALU.mult)
                        step(last)
                    TT(xs, xs, ga, ALU.add).then_inc(S("residual"), 1)
            dve.wait_ge(S("rstd_ready"), 2)
            for t in range(NT):
                TSC(yfin[0:ROWS[t], t, :], x2[0:ROWS[t], t, :], rs[0:ROWS[t], t:t + 1], None, ALU.mult)\
                    .then_inc(S("xn2_ready"), 1)
            dve.wait_ge(S("evac2"), 2 * KD + 12)
            modulate(xnT2, coefF, 24, 6, "h2_ready")

            def leave_rest(t, part):
                n = ROWS[t]
                dve.wait_ge(S(f"part{part}"), t + 1)
                rest = yfin[0:n, t, :]
                before = rest if part else flat(2 * (t % 2), D)[0:n]
                TT(rest, before, h2p[0:n, part, t, :], ALU.subtract).then_inc(S(f"rest{part}"), 1)

            leave_rest(0, 0)
            leave_rest(1, 0)
            leave_rest(0, 1)
            dve.wait_ge(S("logits"), 1)
            for t in range(NT):
                n = ROWS[t]
                TT(logit[0:n, t, :], psum[0:n, 7, 32 * t:32 * t + 32], brout[0:n, :], ALU.add)\
                    .then_inc(S("logits_biased"), 1)
            leave_rest(2, 0)
            dve.wait_ge(S("logits_biased"), NT)
            for t in range(NT):
                last = dve.max(top8[0:ROWS[t], t, :], logit[0:ROWS[t], t, :])
            step(last)
            for t in range(NT):
                dve.max_index(idx8[0:ROWS[t], t, :], top8[0:ROWS[t], t, :], logit[0:ROWS[t], t, :])
                last = TSC(nmax[0:ROWS[t], t:t + 1], top8[0:ROWS[t], t, 0:1], -1.0, None, ALU.mult)
            last.then_inc(S("softmax_in"), 1)
            dve.wait_ge(S("softmax_in"), 1)
            for t in range(NT):
                last = dve.tensor_copy(idxf[0:ROWS[t], t, :], idx8[0:ROWS[t], t, :])
            step(last)
            for k in range(4):
                for t in range(NT):
                    n = ROWS[t]
                    if k == 0:
                        last = TSC(route[0:n, t, :], K("eidx")[0:n, :], idxf[0:n, t, 0:1], None, ALU.is_equal)
                    else:
                        last = STT(route[0:n, t, :], K("eidx")[0:n, :], idxf[0:n, t, k:k + 1], route[0:n, t, :],
                                   ALU.is_equal, ALU.add)
                if k < 3:
                    step(last)
            last.then_inc(S("route_ready"), 1)
            leave_rest(1, 1)
            leave_rest(2, 1)
            step(dve.memset(pos, 0.0))
            dve.wait_ge(S("places"), 1)
            for t in range(NT):
                n = ROWS[t]
                last = TT(pos[0:n, t, 0:NE], psum[0:n, 6, 32 * t:32 * t + 32], route[0:n, t, :], ALU.mult)
            step(last)
            step(TSC(pos, pos, -1.0, None, ALU.add))
            step(dve.tensor_copy(counts[:, 0:NE], psum[:, 6, 96:128]))
            step(dve.reduce_max(counts[:, NE:NE + 1], counts[:, 0:NE], X))
            dve.tensor_copy(counts_i, counts).then_inc(S("counts_ready"), 1)
            dve.wait_ge(S("P_zero"), 1)

            def one_hot(r, e, i):
                if not isinstance(i, int) or i > 0:
                    dve.wait_ge(S("gathered"), i)
                sl = K("slots")[:, bass.ds(r * 128, 128)] if not isinstance(r, int) else \
                    K("slots")[:, r * 128:r * 128 + 128]
                for t in range(NT):
                    n = ROWS[t]
                    last = TSC(P[0:n, t, :], sl[0:n, :], pos[0:n, t, bass.ds(e, 1)], None, ALU.is_equal)
                last.then_inc(S("P_ready"), 1)

            def expert(r, e, it, count):
                ig = r * (NE + 1) + e
                one_hot(r, e + 1, ig + 1)

                def weighted(slots):
                    first = r * 128 if isinstance(r, int) else None
                    sl = K("slots")[:, bass.ds(r * 128, 128)] if first is None else K("slots")[:, first:first + slots]
                    for t in range(NT):
                        n = ROWS[t]
                        last = TSC(Pg[0:n, t, :].rearrange("p (q s) -> p q s", s=slots),
                                   sl[0:n, :].unsqueeze(1).to_broadcast([n, 128 // slots, slots]),
                                   pos[0:n, t, bass.ds(e, 1)], gate[0:n, t, bass.ds(e, 1)], ALU.is_equal, ALU.mult)
                    last.then_inc(S("Pg_ready"), 1)

                def swiglu(slots):
                    n = 8 * slots
                    g_, s_, l_ = (v.rearrange("p u n -> p (u n)")[:, 0:n] for v in (gt_, sg, li))
                    gate_in = flat(0, n)
                    lin_in = psum[:, 0, 256:512] if slots == 32 else flat(slots // 64, n)
                    dve.wait_ge(S("up_done"), it + 1)
                    TSC(g_, gate_in, 7.0, None, ALU.min).then_inc(S("gate_ready"), 1)
                    TSC(l_, lin_in, 7.0, -7.0, ALU.min, ALU.max).then_inc(S("lin_clipped"), 1)
                    dve.wait_ge(S("lin_clipped"), it + 1)
                    dve.wait_ge(S("gate_ready"), it + 1)
                    STT(l_, l_, 1.0, g_, ALU.add, ALU.mult).then_inc(S("lin_gated"), 1)
                    dve.wait_ge(S("lin_gated"), it + 1)
                    dve.wait_ge(S("sig_ready"), it + 1)
                    TT(g_, l_, s_, ALU.mult).then_inc(S("act_ready"), 1)

                by_size(dve, count, weighted)
                by_size(dve, count, swiglu)
                add_scattered(it)

            def add_scattered(it):
                for t in range(NT):
                    dve.wait_ge(S("scattered"), 3 * it + t + 1)
                    v = acc[:, t, :] if t < 2 else acc[:, 2, 0:512]
                    src = flat((6, 4, 6)[t], D if t < 2 else 512)
                    TT(v, v, src, ALU.add).then_inc(S("added"), 1)
                dve.wait_ge(S("added"), 3 * it + 4)

            def finish(its):
                finish_step = chained(dve, "finish_step")
                finish_step(dve.tensor_copy(acc[0:64, 2, 512:D], acc[64:128, 2, 0:512]))
                for t in range(NT):
                    n = ROWS[t]
                    finish_step(TT(acc[0:n, t, :], acc[0:n, t, :], gateF[0:n, t, :], ALU.mult))
                    finish_step(TT(x2[0:n, t, :], x2[0:n, t, :], acc[0:n, t, :], ALU.add))
                for t in range(NT):
                    n = ROWS[t]
                    dve.wait_ge(S("scattered"), 3 * its + t + 1)
                    if t < 2:
                        TT(acc[:, t, :], flat(6 - 2 * t, D), gateF[:, t, :], ALU.mult).then_inc(S("added"), 1)
                        dve.wait_ge(S("added"), 3 * its + 2 + t)
                    else:
                        for u in range(2):
                            cols = slice(512 * u, 512 * u + 512)
                            last = TT(acc[0:64, 2, cols], psum[64 * u:64 * u + 64, 6, :], gateF[0:64, 2, cols], ALU.mult)
                        finish_step(last)
                    TT(x2[0:n, t, :], x2[0:n, t, :], acc[0:n, t, :], ALU.add).then_inc(S("x3_ready"), 1)

            one_hot(0, 0, 0)
            dve.wait_ge(S("route_ready"), 1)
            dve.wait_ge(S("softmax_exp"), 1)
            for t in range(NT):
                n = ROWS[t]
                step(TT(pexp[0:n, t, :], pexp[0:n, t, :], route[0:n, t, :], ALU.mult))
                step(dve.reduce_sum(nmax[0:n, t:t + 1], pexp[0:n, t, :], X))
                step(dve.reciprocal(nmax[0:n, t:t + 1], nmax[0:n, t:t + 1]))
                step(TSC(gate[0:n, t, 0:NE], pexp[0:n, t, :], nmax[0:n, t:t + 1], None, ALU.mult))
            for part in range(3):
                dve.wait_ge(S(f"part{part}"), NT)
            dve.memset(acc, 0.0).then_inc(S("added"), 1)
            dve.wait_ge(S("added"), 1)
            with dve.Fori(0, NE) as e:
                count = dve.value_load(counts_i[0:1, bass.ds(e, 1)], min_val=0, max_val=NTOK)
                expert(0, e, e, count)
            most = dve.value_load(counts_i[0:1, NE:NE + 1], min_val=0, max_val=NTOK)
            with dve.If(most > BIG_BLOCK):
                with dve.Fori(1, ROUNDS) as r:
                    one_hot(r, 0, r * (NE + 1))
                    with dve.Fori(0, NE) as e:
                        expert(r, e, r * NE + e, None)
                finish(NE * ROUNDS)
            with dve.Else():
                finish(NE)
            dve.wait_ge(S("gfin_in"), 16)
            for t in range(NT):
                n = ROWS[t]
                dve.wait_ge(S("rstd3"), t + 1)
                STT(x2[0:n, t, :], x2[0:n, t, :], rs[0:n, t:t + 1], gfin.rearrange("p u n -> p (u n)")[0:n, :],
                    ALU.mult, ALU.mult).then_inc(S("y_final"), 1)


_OUTS = [("y_prompt", (1, SEQ, D)), ("y_sample", (NSEQ, TS, D)),
         ("ret_p", (1, 1, H, HD, HD)), ("c_p", (1, 1, H, HD, HD)), ("n_p", (1, 1, H, HD)), ("m_p", (1, 1, H)),
         ("conv_p", (1, 1, 3, D)),
         ("ret_s", (1, NSEQ, H, HD, HD)), ("c_s", (1, NSEQ, H, HD, HD)), ("n_s", (1, NSEQ, H, HD)),
         ("m_s", (1, NSEQ, H)), ("conv_s", (1, NSEQ, 3, D))]


def kernel(**inputs):
    import concourse.bacc as bacc
    from concourse.bass_utils import run_bass_kernel_spmd

    nc = bacc.Bacc("TRN2", target_bir_lowering=False, num_devices=1)
    arrays, aps = {}, {}

    def give(name, v):
        v = np.ascontiguousarray(v)
        arrays[f"in_{name}"] = v
        aps[name] = nc.dram_tensor(f"in_{name}", v.shape, mybir.dt.from_np(v.dtype), kind="ExternalInput").ap()

    for name, v in inputs.items():
        give(name, v)
    give("tables", np.concatenate(list(constant_tables().values()), axis=1))
    give("selectors", gate_selectors())
    for name, shape in _OUTS:
        aps[name] = nc.dram_tensor(f"out_{name}", shape, mybir.dt.float32, kind="ExternalOutput").ap()
    build(nc, aps)
    r = run_bass_kernel_spmd(nc, [arrays], core_ids=[0])
    return tuple(r.results[0][f"out_{name}"] for name, _ in _OUTS)
```
